# Optimizing a Trainium2 kernel written in Bass

```python
import jax, jax.numpy as jnp
from jax import lax
import numpy as np

D_MODEL = 1024
BATCH = 1
SEQ = 512
DEPTH = 2

GRID_W = 64
NA_HEADS = 4
NA_HEAD_DIM = 64
NA_KH = 8
NA_KW = 16
NA_QB = 16
MLA_HEADS = 4
MLA_Q_LORA = 256
MLA_KV_LORA = 128
MLA_NOPE = 64
MLA_ROPE = 32
MLA_V = 64
GQA_HEADS = 8
GQA_KV_HEADS = 2
GQA_HEAD_DIM = 64
N_BRANCHES = 3
FFN_HIDDEN = -(-8 * D_MODEL // (3 * 256)) * 256
Q_BLOCK = 128
ROPE_THETA = 10000.0
AXIAL_THETA = 10000.0
NORM_EPS = 1e-6
N_MOD = 6


def _in_splits():
    return ([NA_HEADS * NA_HEAD_DIM] * 3
            + [MLA_Q_LORA, MLA_KV_LORA, MLA_ROPE]
            + [GQA_HEADS * GQA_HEAD_DIM, GQA_KV_HEADS * GQA_HEAD_DIM, GQA_KV_HEADS * GQA_HEAD_DIM]
            + [D_MODEL] * N_BRANCHES)

def _in_cols():
    return int(sum(_in_splits()))

def rms_norm(x, g):
    xf = x.astype(jnp.float32)
    y = xf * lax.rsqrt(jnp.mean(xf * xf, axis=-1, keepdims=True) + NORM_EPS)
    return (y * g.astype(jnp.float32)).astype(x.dtype)

def rope(x, pos, theta):
    d = x.shape[-1]
    half = d // 2
    inv_freq = 1.0 / (theta ** (jnp.arange(half, dtype=jnp.float32) / half))
    ang = pos[:, None] * inv_freq[None, :]
    ang = ang.reshape((ang.shape[0],) + (1,) * (x.ndim - 3) + (half,))
    cos, sin = jnp.cos(ang), jnp.sin(ang)
    xf = x.astype(jnp.float32)
    x1, x2 = xf[..., :half], xf[..., half:]
    return jnp.concatenate([x1 * cos - x2 * sin, x2 * cos + x1 * sin], axis=-1).astype(x.dtype)

def axial_rope(x, row, col):
    h = x.shape[-1] // 2
    return jnp.concatenate([rope(x[..., :h], row, AXIAL_THETA), rope(x[..., h:], col, AXIAL_THETA)], axis=-1)

def blocked_attention(q, k, v, scale):
    B, S, KVH, G, dk = q.shape
    dv = v.shape[-1]
    nb = S // Q_BLOCK
    qb = jnp.moveaxis(q.reshape(B, nb, Q_BLOCK, KVH, G, dk), 1, 0)

    def one_block(qi):
        s = jnp.einsum('bqkgd,bskd->bkgqs', qi, k, preferred_element_type=jnp.float32) * scale
        p = jax.nn.softmax(s, axis=-1)
        return jnp.einsum('bkgqs,bskd->bqkgd', p.astype(v.dtype), v)

    o = lax.map(one_block, qb)
    return jnp.moveaxis(o, 0, 1).reshape(B, S, KVH * G * dv)

def neighborhood_attention(q, k, v, rpb):
    B, S, H, d = q.shape
    rows = S // GRID_W
    kh = min(NA_KH, rows)
    kw = NA_KW
    n_cb = GRID_W // NA_QB
    band = NA_QB + kw
    scale = d ** -0.5
    qg = q.reshape(B, rows, GRID_W, H, d)
    kg = k.reshape(B, rows, GRID_W, H, d)
    vg = v.reshape(B, rows, GRID_W, H, d)

    cb_start = jnp.clip(jnp.arange(n_cb) * NA_QB - kw // 2, 0, GRID_W - band)
    band_cols = cb_start[:, None] + jnp.arange(band)[None, :]
    q_cols = (jnp.arange(n_cb) * NA_QB)[:, None] + jnp.arange(NA_QB)[None, :]
    win_start = jnp.clip(q_cols - kw // 2, 0, GRID_W - kw)
    bc = band_cols[:, None, :]
    col_valid = (bc >= win_start[..., None]) & (bc < win_start[..., None] + kw)
    col_off = jnp.clip(bc - q_cols[..., None], -(kw - 1), kw - 1) + (kw - 1)
    rpb_cols = rpb[:, :, col_off]

    def one_row(r):
        rs = jnp.clip(r - kh // 2, 0, rows - kh)
        k_rows = lax.dynamic_slice_in_dim(kg, rs, kh, axis=1)
        v_rows = lax.dynamic_slice_in_dim(vg, rs, kh, axis=1)
        k_band = k_rows[:, :, band_cols]
        v_band = v_rows[:, :, band_cols]
        q_row = lax.dynamic_index_in_dim(qg, r, axis=1, keepdims=False).reshape(B, n_cb, NA_QB, H, d)
        s = jnp.einsum('bnqhd,bknjhd->bhnqkj', q_row, k_band, preferred_element_type=jnp.float32) * scale
        row_off = rs + jnp.arange(kh) - r + (NA_KH - 1)
        bias = jnp.transpose(rpb_cols[:, row_off], (0, 2, 3, 1, 4))
        s = s + bias[None].astype(jnp.float32)
        s = jnp.where(col_valid[None, None, :, :, None, :], s, -jnp.inf)
        p = jax.nn.softmax(s.reshape(B, H, n_cb, NA_QB, kh * band), axis=-1)
        p = p.reshape(B, H, n_cb, NA_QB, kh, band)
        o = jnp.einsum('bhnqkj,bknjhd->bnqhd', p.astype(v.dtype), v_band)
        return o.reshape(B, GRID_W, H, d)

    out = lax.map(one_row, jnp.arange(rows))
    return jnp.moveaxis(out, 0, 1).reshape(B, S, H * d)

def hybrid_layer(x, c, ada_w, ada_b, norm_mix_g, norm_ffn_g, w_in, na_rpb,
                 mla_q_norm_g, mla_kv_norm_g, mla_w_uq, mla_w_ukv, gqa_q_norm_g, gqa_k_norm_g,
                 w_br_na, w_br_mla, w_br_gqa, w_out, ffn_w_gate_up, ffn_w_down, pos_t, pos_row, pos_col):
    B, S, D = x.shape
    mod = jax.nn.silu(c) @ ada_w + ada_b
    sh_m, sc_m, g_m, sh_f, sc_f, g_f = [m[:, None, :] for m in jnp.split(mod, N_MOD, axis=-1)]

    h = rms_norm(x, norm_mix_g) * (1 + sc_m) + sh_m
    proj = h @ w_in
    idx = [int(i) for i in np.cumsum(_in_splits())[:-1]]
    (qa, ka, va, cq, ckv, kr, qc, kc, vc, ga, gb, gc) = jnp.split(proj, idx, axis=-1)

    o_na = neighborhood_attention(qa.reshape(B, S, NA_HEADS, NA_HEAD_DIM),
                                  ka.reshape(B, S, NA_HEADS, NA_HEAD_DIM),
                                  va.reshape(B, S, NA_HEADS, NA_HEAD_DIM), na_rpb)

    q_b = (rms_norm(cq, mla_q_norm_g) @ mla_w_uq).reshape(B, S, MLA_HEADS, MLA_NOPE + MLA_ROPE)
    q_nope, q_pe = q_b[..., :MLA_NOPE], rope(q_b[..., MLA_NOPE:], pos_t, ROPE_THETA)
    kv_b = (rms_norm(ckv, mla_kv_norm_g) @ mla_w_ukv).reshape(B, S, MLA_HEADS, MLA_NOPE + MLA_V)
    k_nope, v_b = kv_b[..., :MLA_NOPE], kv_b[..., MLA_NOPE:]
    k_pe = jnp.broadcast_to(rope(kr, pos_t, ROPE_THETA)[:, :, None, :], (B, S, MLA_HEADS, MLA_ROPE))
    q_full = jnp.concatenate([q_nope, q_pe], axis=-1)[:, :, :, None, :]
    k_full = jnp.concatenate([k_nope, k_pe], axis=-1)
    o_mla = blocked_attention(q_full, k_full, v_b, (MLA_NOPE + MLA_ROPE) ** -0.5)

    q_c = axial_rope(rms_norm(qc.reshape(B, S, GQA_HEADS, GQA_HEAD_DIM), gqa_q_norm_g), pos_row, pos_col)
    k_c = axial_rope(rms_norm(kc.reshape(B, S, GQA_KV_HEADS, GQA_HEAD_DIM), gqa_k_norm_g), pos_row, pos_col)
    v_c = vc.reshape(B, S, GQA_KV_HEADS, GQA_HEAD_DIM)
    q_c = q_c.reshape(B, S, GQA_KV_HEADS, GQA_HEADS // GQA_KV_HEADS, GQA_HEAD_DIM)
    o_gqa = blocked_attention(q_c, k_c, v_c, GQA_HEAD_DIM ** -0.5)

    merged = (jax.nn.sigmoid(ga) * (o_na @ w_br_na)
              + jax.nn.sigmoid(gb) * (o_mla @ w_br_mla)
              + jax.nn.sigmoid(gc) * (o_gqa @ w_br_gqa))
    x = x + g_m * (merged @ w_out)

    h = rms_norm(x, norm_ffn_g) * (1 + sc_f) + sh_f
    gate, up = jnp.split(h @ ffn_w_gate_up, 2, axis=-1)
    x = x + g_f * ((jax.nn.silu(gate) * up) @ ffn_w_down)
    return x

def first_inputs(seed: int = 0) -> dict:
    key = jax.random.key(seed)
    ks = jax.random.split(key, 24)
    f32 = jnp.float32

    def w(k, shape, fan_in):
        return jax.random.normal(k, shape, f32) * fan_in ** -0.5

    def gain(k, shape):
        return 1.0 + 0.02 * jax.random.normal(k, shape, f32)

    L, D = DEPTH, D_MODEL
    return {
        "x": jax.random.normal(ks[0], (BATCH, SEQ, D), f32),
        "c": jax.random.normal(ks[1], (BATCH, D), f32),
        "ada_w": w(ks[2], (L, D, N_MOD * D), D),
        "ada_b": 0.02 * jax.random.normal(ks[3], (L, N_MOD * D), f32),
        "norm_mix_g": gain(ks[4], (L, D)),
        "norm_ffn_g": gain(ks[5], (L, D)),
        "w_in": w(ks[6], (L, D, _in_cols()), D),
        "na_rpb": 0.1 * jax.random.normal(ks[7], (L, NA_HEADS, 2 * NA_KH - 1, 2 * NA_KW - 1), f32),
        "mla_q_norm_g": gain(ks[8], (L, MLA_Q_LORA)),
        "mla_kv_norm_g": gain(ks[9], (L, MLA_KV_LORA)),
        "mla_w_uq": w(ks[10], (L, MLA_Q_LORA, MLA_HEADS * (MLA_NOPE + MLA_ROPE)), MLA_Q_LORA),
        "mla_w_ukv": w(ks[11], (L, MLA_KV_LORA, MLA_HEADS * (MLA_NOPE + MLA_V)), MLA_KV_LORA),
        "gqa_q_norm_g": gain(ks[12], (L, GQA_HEAD_DIM)),
        "gqa_k_norm_g": gain(ks[13], (L, GQA_HEAD_DIM)),
        "w_br_na": w(ks[14], (L, NA_HEADS * NA_HEAD_DIM, D), NA_HEADS * NA_HEAD_DIM),
        "w_br_mla": w(ks[15], (L, MLA_HEADS * MLA_V, D), MLA_HEADS * MLA_V),
        "w_br_gqa": w(ks[16], (L, GQA_HEADS * GQA_HEAD_DIM, D), GQA_HEADS * GQA_HEAD_DIM),
        "w_out": w(ks[17], (L, D, D), D),
        "ffn_w_gate_up": w(ks[18], (L, D, 2 * FFN_HIDDEN), D),
        "ffn_w_down": w(ks[19], (L, FFN_HIDDEN, D), FFN_HIDDEN),
        "final_norm_g": gain(ks[20], (D,)),
    }

def first_block(x, c, ada_w, ada_b, norm_mix_g, norm_ffn_g, w_in, na_rpb, mla_q_norm_g, mla_kv_norm_g,
              mla_w_uq, mla_w_ukv, gqa_q_norm_g, gqa_k_norm_g, w_br_na, w_br_mla, w_br_gqa, w_out,
              ffn_w_gate_up, ffn_w_down, final_norm_g):
    S = x.shape[1]
    t = jnp.arange(S, dtype=jnp.int32)
    pos_t = t.astype(jnp.float32)
    pos_row = (t // GRID_W).astype(jnp.float32)
    pos_col = (t % GRID_W).astype(jnp.float32)
    for l in range(DEPTH):
        x = hybrid_layer(x, c, ada_w[l], ada_b[l], norm_mix_g[l], norm_ffn_g[l], w_in[l], na_rpb[l],
                         mla_q_norm_g[l], mla_kv_norm_g[l], mla_w_uq[l], mla_w_ukv[l],
                         gqa_q_norm_g[l], gqa_k_norm_g[l], w_br_na[l], w_br_mla[l], w_br_gqa[l], w_out[l],
                         ffn_w_gate_up[l], ffn_w_down[l], pos_t, pos_row, pos_col)
    return rms_norm(x, final_norm_g)


DEPTH_2 = 1

CHUNK = 64
EPS = 1e-6
D_A = D_MODEL
CONV_A = 3
D_B = D_MODEL
LRU_HEADS = 16
LRU_BW = D_B // LRU_HEADS
CONV_B = 4
LRU_C = 8.0
D_C = D_MODEL
RWKV_HEAD = 64
RWKV_HEADS = D_C // RWKV_HEAD
R_W = 64
R_A = 64
R_V = 32
R_G = 128
LNX_EPS = RWKV_HEAD * 1e-5
D_FF = 4 * D_MODEL
N_BRANCH = 3
COLS_A = 3 * D_A
COLS_B = 2 * D_B
COLS_GATE = N_BRANCH * D_MODEL
COLS_C = 3 * D_C + R_W + R_A + R_G
N_IN = COLS_A + COLS_B + COLS_GATE + COLS_C


def _split(t, sizes):
    out, o = [], 0
    for s in sizes:
        out.append(t[..., o:o + s])
        o += s
    return out

def rms_norm_2(x, g):
    xf = x.astype(jnp.float32)
    y = xf * lax.rsqrt(jnp.mean(xf * xf, axis=-1, keepdims=True) + EPS)
    return (y * g.astype(jnp.float32)).astype(x.dtype)

def causal_dwconv(x, w, b=None):
    K = w.shape[0]
    S = x.shape[1]
    xp = jnp.pad(x, ((0, 0), (K - 1, 0), (0, 0)))
    y = xp[:, K - 1:K - 1 + S] * w[K - 1]
    for j in range(K - 1):
        y = y + xp[:, j:j + S] * w[j]
    return y if b is None else y + b

def token_shift(p, mu):
    prev = jnp.pad(p, ((0, 0), (1, 0), (0, 0)))[:, :-1]
    return p + (prev - p) * mu

def rg_lru(x, w_a, b_a, w_i, b_i, a_param):
    Bsz, S, C = x.shape
    f32 = jnp.float32
    xb = x.reshape(Bsz, S, LRU_HEADS, LRU_BW)
    gate_a = jax.nn.sigmoid((jnp.einsum('bshi,hij->bshj', xb, w_a).reshape(Bsz, S, C) + b_a).astype(f32))
    gate_i = jax.nn.sigmoid((jnp.einsum('bshi,hij->bshj', xb, w_i).reshape(Bsz, S, C) + b_i).astype(f32))
    log_a = -LRU_C * gate_a * jax.nn.softplus(a_param.astype(f32))
    a = jnp.exp(log_a)
    mult = jnp.sqrt(-jnp.expm1(2.0 * log_a))
    mult = jnp.where(jnp.arange(S)[None, :, None] == 0, 1.0, mult)
    u = x.astype(f32) * gate_i * mult

    def combine(left, right):
        a_l, u_l = left
        a_r, u_r = right
        return a_l * a_r, a_r * u_l + u_r

    _, h = lax.associative_scan(combine, (a, u), axis=1)
    return h.astype(x.dtype)

def rwkv7_recurrence(r, decay, k, v, kk, a):
    Bsz, S, H, N = r.shape
    nc = S // CHUNK

    def to_chunks(t):
        return t.reshape(Bsz, nc, CHUNK, H, N).transpose(1, 2, 0, 3, 4)

    def step(state, inp):
        r_t, w_t, k_t, v_t, kk_t, a_t = inp
        sa = jnp.einsum('bhvk,bhk->bhv', state, -kk_t)
        state = (state * w_t[:, :, None, :]
                 + sa[..., None] * (kk_t * a_t)[:, :, None, :]
                 + v_t[..., None] * k_t[:, :, None, :])
        y_t = jnp.einsum('bhvk,bhk->bhv', state, r_t)
        return state, y_t

    def chunk_step(state, chunk_inp):
        return lax.scan(step, state, chunk_inp)

    state0 = jnp.zeros((Bsz, H, N, N), jnp.float32)
    inputs = (to_chunks(r), to_chunks(decay), to_chunks(k), to_chunks(v), to_chunks(kk), to_chunks(a))
    _, y = lax.scan(chunk_step, state0, inputs)
    return y.transpose(2, 0, 1, 3, 4).reshape(Bsz, S, H, N)

def rwkv7_mix(pc, h, v_first, w0, w2, a0, a2, g2, k_k, k_a, r_k, lnx_g, lnx_b, vres):
    f32 = jnp.float32
    r, k, v, xw, xa, xg = _split(pc, (D_C, D_C, D_C, R_W, R_A, R_G))
    w_log = -jax.nn.softplus(-(w0 + jnp.tanh(xw) @ w2).astype(f32)) - 0.5
    decay = jnp.exp(-jnp.exp(w_log))
    if vres is None:
        v_first = v
    else:
        v0, v1, v2 = vres
        v = v + (v_first - v) * jax.nn.sigmoid(v0 + (h @ v1) @ v2)
    a = jax.nn.sigmoid(a0 + xa @ a2)
    g = jax.nn.sigmoid(xg) @ g2

    def heads(t):
        return t.reshape(t.shape[:-1] + (RWKV_HEADS, RWKV_HEAD)).astype(f32)

    kk = heads(k * k_k)
    kk = kk / jnp.maximum(jnp.sqrt(jnp.sum(kk * kk, axis=-1, keepdims=True)), 1e-12)
    k = k * (1.0 + (a - 1.0) * k_a)
    rh, kh, vh, ah = heads(r), heads(k), heads(v), heads(a)
    y = rwkv7_recurrence(rh, heads(decay), kh, vh, kk, ah)
    mu = jnp.mean(y, axis=-1, keepdims=True)
    var = jnp.mean(jnp.square(y - mu), axis=-1, keepdims=True)
    y = (y - mu) * lax.rsqrt(var + LNX_EPS)
    y = y + jnp.sum(rh * kh * r_k.astype(f32), axis=-1, keepdims=True) * vh
    y = y.reshape(y.shape[:2] + (D_C,))
    return y, g, v_first

def second_inputs(seed: int = 0) -> dict:
    key = jax.random.key(seed)
    ks = iter(jax.random.split(key, 48))
    L = DEPTH_2

    def nrm(shape, scale):
        return jax.random.normal(next(ks), shape, jnp.float32) * scale

    def uni(shape, lo, hi):
        return jax.random.uniform(next(ks), shape, jnp.float32, lo, hi)

    rad = uni((L, D_B), 0.9, 0.999)
    lru_a_param = jnp.log(jnp.expm1(-jnp.log(rad)))
    LV = max(L - 1, 0)
    return {
        "x": nrm((BATCH, SEQ, D_MODEL), 1.0),
        "norm1_g": 1.0 + nrm((L, D_MODEL), 0.05),
        "w_in": nrm((L, D_MODEL, N_IN), D_MODEL ** -0.5),
        "merge_b": nrm((L, COLS_GATE), 0.01),
        "conv_a_w": nrm((L, CONV_A, D_A), CONV_A ** -0.5),
        "lru_conv_w": nrm((L, CONV_B, D_B), CONV_B ** -0.5),
        "lru_conv_b": nrm((L, D_B), 0.01),
        "lru_wa": nrm((L, LRU_HEADS, LRU_BW, LRU_BW), LRU_BW ** -0.5),
        "lru_ba": nrm((L, D_B), 0.01),
        "lru_wi": nrm((L, LRU_HEADS, LRU_BW, LRU_BW), LRU_BW ** -0.5),
        "lru_bi": nrm((L, D_B), 0.01),
        "lru_a_param": lru_a_param,
        "rwkv_mu": uni((L, COLS_C), 0.0, 1.0),
        "rwkv_w0": uni((L, D_C), -6.0, 1.0),
        "rwkv_w2": nrm((L, R_W, D_C), 0.1 * R_W ** -0.5),
        "rwkv_a0": nrm((L, D_C), 0.1),
        "rwkv_a2": nrm((L, R_A, D_C), 0.1 * R_A ** -0.5),
        "rwkv_g2": nrm((L, R_G, D_C), R_G ** -0.5),
        "rwkv_kk": 0.85 + nrm((L, D_C), 0.05),
        "rwkv_ka": 1.0 + nrm((L, D_C), 0.05),
        "rwkv_rk": nrm((L, RWKV_HEADS, RWKV_HEAD), 0.1),
        "rwkv_lnx_g": 1.0 + nrm((L, D_C), 0.05),
        "rwkv_lnx_b": nrm((L, D_C), 0.01),
        "rwkv_v0": 1.0 + nrm((LV, D_C), 0.1),
        "rwkv_v1": nrm((LV, D_MODEL, R_V), D_MODEL ** -0.5),
        "rwkv_v2": nrm((LV, R_V, D_C), 0.1 * R_V ** -0.5),
        "w_out": nrm((L, D_MODEL, D_MODEL), D_MODEL ** -0.5),
        "norm2_g": 1.0 + nrm((L, D_MODEL), 0.05),
        "mlp_w1": nrm((L, D_MODEL, D_FF), D_MODEL ** -0.5),
        "mlp_w2": nrm((L, D_FF, D_MODEL), D_FF ** -0.5),
        "final_g": 1.0 + nrm((D_MODEL,), 0.05),
    }

def second_block(x, norm1_g, w_in, merge_b, conv_a_w, lru_conv_w, lru_conv_b, lru_wa, lru_ba, lru_wi,
              lru_bi, lru_a_param, rwkv_mu, rwkv_w0, rwkv_w2, rwkv_a0, rwkv_a2, rwkv_g2, rwkv_kk,
              rwkv_ka, rwkv_rk, rwkv_lnx_g, rwkv_lnx_b, rwkv_v0, rwkv_v1, rwkv_v2, w_out, norm2_g,
              mlp_w1, mlp_w2, final_g):
    v_first = None
    for l in range(DEPTH_2):
        h = rms_norm_2(x, norm1_g[l])
        p = h @ w_in[l]
        pa, pb, pg, pc = _split(p, (COLS_A, COLS_B, COLS_GATE, COLS_C))

        b_a, c_a, x_a = _split(pa, (D_A, D_A, D_A))
        y_a = b_a * causal_dwconv(c_a * x_a, conv_a_w[l])

        x_b, g_b = _split(pb, (D_B, D_B))
        u = causal_dwconv(x_b, lru_conv_w[l], lru_conv_b[l])
        y_b = rg_lru(u, lru_wa[l], lru_ba[l], lru_wi[l], lru_bi[l], lru_a_param[l]) * jax.nn.gelu(g_b, approximate=True)

        pc = token_shift(pc, rwkv_mu[l])
        vres = None if l == 0 else (rwkv_v0[l - 1], rwkv_v1[l - 1], rwkv_v2[l - 1])
        f32 = jnp.float32
        r, k, v, xw, xa, xg = _split(pc, (D_C, D_C, D_C, R_W, R_A, R_G))
        w_log = -jax.nn.softplus(-(rwkv_w0[l] + jnp.tanh(xw) @ rwkv_w2[l]).astype(f32)) - 0.5
        decay = jnp.exp(-jnp.exp(w_log))
        if vres is None:
            v_first = v
        else:
            v0, v1, v2 = vres
            v = v + (v_first - v) * jax.nn.sigmoid(v0 + (h @ v1) @ v2)
        a = jax.nn.sigmoid(rwkv_a0[l] + xa @ rwkv_a2[l])
        g_c = jax.nn.sigmoid(xg) @ rwkv_g2[l]
        hs = x.shape[:2] + (RWKV_HEADS, RWKV_HEAD)
        kk = (k * rwkv_kk[l]).astype(f32).reshape(hs)
        kk = kk / jnp.maximum(jnp.sqrt(jnp.sum(kk * kk, axis=-1, keepdims=True)), 1e-12)
        k = k * (1.0 + (a - 1.0) * rwkv_ka[l])
        rh = r.astype(f32).reshape(hs)
        kh = k.astype(f32).reshape(hs)
        vh = v.astype(f32).reshape(hs)
        ah = a.astype(f32).reshape(hs)
        yc = rwkv7_recurrence(rh, decay.reshape(hs), kh, vh, kk, ah)
        mu = jnp.mean(yc, axis=-1, keepdims=True)
        var = jnp.mean(jnp.square(yc - mu), axis=-1, keepdims=True)
        yc = ((yc - mu) * lax.rsqrt(var + LNX_EPS)).reshape(x.shape[:2] + (D_C,))
        yc = yc * rwkv_lnx_g[l].astype(f32) + rwkv_lnx_b[l].astype(f32)
        bonus = jnp.sum(rh * kh * rwkv_rk[l].astype(f32), axis=-1, keepdims=True) * vh
        yc = yc + bonus.reshape(x.shape[:2] + (D_C,))
        y_c = (yc * g_c.astype(f32)).astype(x.dtype)

        gate_a, gate_b, gate_c = _split(jax.nn.sigmoid(pg + merge_b[l]), (D_MODEL, D_MODEL, D_MODEL))
        m = gate_a * y_a + gate_b * y_b + gate_c * y_c
        x = x + m @ w_out[l]

        h2 = rms_norm_2(x, norm2_g[l])
        x = x + jnp.square(jax.nn.relu(h2 @ mlp_w1[l])) @ mlp_w2[l]
    return rms_norm_2(x, final_g)


def setup_inputs(seed=0):
    out = dict(first_inputs(seed))
    for name, value in second_inputs(seed + 1).items():
        if name != "x":
            out[name + "_2"] = value
    return out


def reference(
    x, c, ada_w, ada_b, norm_mix_g, norm_ffn_g, w_in, na_rpb, mla_q_norm_g, mla_kv_norm_g,
    mla_w_uq, mla_w_ukv, gqa_q_norm_g, gqa_k_norm_g, w_br_na, w_br_mla, w_br_gqa, w_out,
    ffn_w_gate_up, ffn_w_down, final_norm_g, norm1_g_2, w_in_2, merge_b_2, conv_a_w_2,
    lru_conv_w_2, lru_conv_b_2, lru_wa_2, lru_ba_2, lru_wi_2, lru_bi_2, lru_a_param_2,
    rwkv_mu_2, rwkv_w0_2, rwkv_w2_2, rwkv_a0_2, rwkv_a2_2, rwkv_g2_2, rwkv_kk_2, rwkv_ka_2,
    rwkv_rk_2, rwkv_lnx_g_2, rwkv_lnx_b_2, rwkv_v0_2, rwkv_v1_2, rwkv_v2_2, w_out_2, norm2_g_2,
    mlp_w1_2, mlp_w2_2, final_g_2,
):
    x = first_block(
        x, c, ada_w, ada_b, norm_mix_g, norm_ffn_g, w_in, na_rpb, mla_q_norm_g, mla_kv_norm_g,
        mla_w_uq, mla_w_ukv, gqa_q_norm_g, gqa_k_norm_g, w_br_na, w_br_mla, w_br_gqa, w_out,
        ffn_w_gate_up, ffn_w_down, final_norm_g,
    )
    return second_block(
        x, norm1_g_2, w_in_2, merge_b_2, conv_a_w_2, lru_conv_w_2, lru_conv_b_2, lru_wa_2,
        lru_ba_2, lru_wi_2, lru_bi_2, lru_a_param_2, rwkv_mu_2, rwkv_w0_2, rwkv_w2_2, rwkv_a0_2,
        rwkv_a2_2, rwkv_g2_2, rwkv_kk_2, rwkv_ka_2, rwkv_rk_2, rwkv_lnx_g_2, rwkv_lnx_b_2,
        rwkv_v0_2, rwkv_v1_2, rwkv_v2_2, w_out_2, norm2_g_2, mlp_w1_2, mlp_w2_2, final_g_2,
    )


_drawn_inputs = setup_inputs


def setup_inputs(seed=0):
    import zlib

    import numpy as np

    out = dict(_drawn_inputs(seed))
    spreads = {}
    factors = {'norm_mix_g': 5.019,
     'na_rpb': 4.078,
     'mla_q_norm_g': 8.0,
     'mla_kv_norm_g': 7.279,
     'gqa_q_norm_g': 8.0,
     'gqa_k_norm_g': 8.0,
     'merge_b_2': 8.0,
     'lru_conv_b_2': 8.0,
     'lru_ba_2': 172.362,
     'lru_bi_2': 64.0,
     'rwkv_w2_2': 8.0,
     'rwkv_a0_2': 5.005,
     'rwkv_a2_2': 4.858,
     'rwkv_lnx_g_2': 4.56,
     'rwkv_lnx_b_2': 33.58}
    for name, (base, spread) in spreads.items():
        noise = np.random.default_rng([zlib.crc32(name.encode()), seed]).standard_normal(out[name].shape)
        drawn = base * np.exp(spread * noise) if base else spread * noise
        out[name] = __import__('jax').numpy.asarray(drawn.astype(out[name].dtype))
    for name, factor in factors.items():
        out[name] = (out[name] * factor).astype(out[name].dtype)
    return out
```

```python
from contextlib import ExitStack, contextmanager

import numpy as np

import concourse.bass as bass
from concourse import mybir

ALU = mybir.AluOpType
ACT = mybir.ActivationFunctionType
AX_X = mybir.AxisListType.X
F32 = mybir.dt.float32
F32R = mybir.dt.float32r

P = 128
S = 512
D = 1024
KD = D // P
DEPTH = 2
GRID = 64
SKEW = 127 + GRID - 1
FFN = 2816
KF = FFN // P
NMOD = 6
EPS = 1e-6
RING = 4
AHEAD = 2

T_IN, T_MLA, T_MERGE, T_OUT, T_GU, T_DOWN = 0, 16, 20, 20 + 4 * KD, 20 + 5 * KD, 20 + 5 * KD + 2 * KF
T_LAYER = T_DOWN + 3 * KD
T_B2 = DEPTH * T_LAYER
T_M, T_SMALL = 12, 4
T_OUT2 = T_B2 + 2 + T_M * KD
T_MLP = T_OUT2 + KD
T_USED = T_MLP + 64
T_TOTAL = -(-T_USED // RING) * RING
P_IN, P_MLA, P_MERGE = 0, 16, 26
P_OUT = P_MERGE + 6 * KD
P_GU = P_OUT + KD
P_DOWN = P_GU + 2 * KF
P_LAYER = P_DOWN + KD
P_B2 = DEPTH * P_LAYER
P_M = 16
P_OUT2 = P_B2 + 2 + P_M * KD
P_MLP = P_OUT2 + KD
C_BANK, C_UNIT = 6, 2

CH = 4
RATE = 0.6065306597126334
LNX_EPS = 64e-5
LEVELS = 6
(W_MUK, W_MUV, W_MUR, W_W0, W_A0, W_KK, W_KA, W_RK, W_LG, W_LB, W_CB, W_CW, W_BA, W_BI, W_AP, W_CA, W_MB
 ) = (0, 1, 2, 3, 4, 5, 6, 7, 8, 9, 10, 11, 15, 16, 17, 18, 21)
W_M = 24
X_N1, X_N2, X_FIN, X_MU, X_F1 = 0, 8, 16, 24, 26
W_X = 34
RW = ([("LT", 0, 0), ("LT", 1, 0), ("L", 0, 0), ("L", 1, 0), ("GB", 0, 0), ("GB", 1, 0),
       ("MT", 0, 0), ("MT", 1, 0), ("GK", 0, 0), ("GK", 1, 0)]
      + [(kind, h, lv) for lv in range(1, LEVELS + 1)
         for kind, h in [("X", 0), ("X", 1)] + [(k, h) for h in range(2) for k in ("T", "TT") if k == "TT" or lv < LEVELS]])
RW_BANK = {"LT": 2, "L": 4, "GB": 6, "MT": 2, "GK": 4, "X": 2, "T": 4, "TT": 6}

ACC, SC, PT, OB, SUM = 0, 2, 4, 6, 7
SH_M, SC_M, G_M, SH_F, SC_F, G_F = (KD * i for i in range(NMOD))
V_MIX, V_FFN, V_CQ, V_CKV, V_GQ, V_GK, V_LAYER = 0, 8, 16, 18, 19, 20, 21
HALF_SWAP = list(range(16, 32)) + list(range(16))


class Count:

    def __init__(self, const=0, terms=()):
        self.const, self.terms = const, tuple(terms)

    def __add__(self, n):
        return Count(self.const + n, self.terms)

    def __sub__(self, n):
        return self + -n

    def at(self, var, coef):
        return Count(self.const, self.terms + ((var, coef),))

    def half(self):
        assert all(c % 2 == 0 for _, c in self.terms)
        return Count(self.const // 2, ((v, c // 2) for v, c in self.terms))

    def mod(self, n):
        assert all(c % n == 0 for _, c in self.terms)
        return self.const % n

    def value(self):
        out = self.const
        for v, c in self.terms:
            out = v * c + out
        return out


class Steps:

    def __init__(self, eng, sem, per_loop, passed):
        self.passed = passed
        self.eng, self.sem, self.at, self.per_loop = eng, sem, Count(0), per_loop

    def __call__(self, ins):
        ins.then_inc(self.sem, 1)
        self.at = self.at + 1

    def sync(self):
        self.eng.wait_ge(self.sem, self.at.value())

    @contextmanager
    def loop(self, name, n, start=0):
        per = self.per_loop.get(name, 0)
        self.eng.sem_inc(self.passed, 1)
        with self.eng.Fori(start, n) as i:
            before = self.at
            self.at = Count(before.const - start * per, before.terms).at(i, per)
            base = self.at.const
            yield i
            made = self.at.const - base
            assert made == per, (name, made)
        self.at = before + (n - start) * per


STEPS = {"mod": 1, "na": 21, "mla": 13, "gqa": 12, "merge": 3, "out": 0, "gu": 2, "down": 0, "layer": 269, "m": 53, "mlp1": 4, "mlp2": 0, "mlp": 16}


def three_passes(mm, out, w_hi, w_lo, r_hi, r_lo, first, last):
    mm(out, w_hi, r_hi, start=first, stop=False)
    mm(out, w_hi, r_lo, start=False, stop=False)
    return mm(out, w_lo, r_hi, start=False, stop=last)


def build(nc, x, c, weights, ada_b, vec1, rpb, vec2_in, vecx_in, tables1, out):
    dram_bias = nc.dram_tensor("bias_rows", (DEPTH * 4 * 15, 127), F32, kind="Internal")
    dram_toeplitz = nc.dram_tensor("bias_toeplitz", (DEPTH * 4, GRID, 15, SKEW), F32, kind="Internal")
    with ExitStack() as ctx:
        def sb(name, shape, dt=F32, into=None):
            return (into or ctx).enter_context(nc.sbuf_tensor(name, shape, dt))

        def sem(name):
            return ctx.enter_context(nc.semaphore(name))

        ps = ctx.enter_context(nc.psum_tensor("ps", [P, 8, S], F32))

        xT = sb("xT", [P, KD, S])
        hR = sb("hR", [P, 2, KD, S], F32R)
        raw = sb("raw", [P, RING, 1024])
        wR = sb("wR", [P, RING, 2, 1024], F32R)
        ident = sb("ident", [P, P])
        ones = sb("ones", [P, P])
        blk = sb("blk", [P, P])
        epsb = sb("epsb", [P, 4])
        sq = sb("sq", [P, 2, S])
        work = sb("work", [P, 4, S])
        vecx = sb("vecx", [P, W_X])
        lm = sb("lm", [P, NMOD * KD])
        gs = sb("gs", [P, 2, KD])
        rt, rs, tmp, hf = (work[:, i, :] for i in range(4))

        region = ExitStack()
        with region:
            mod = sb("mod", [P, DEPTH * NMOD * KD], into=region)
            adab = sb("adab", [P, DEPTH * NMOD * KD], into=region)
            vl = sb("vl", [P, DEPTH * V_LAYER], into=region)
            lvec = sb("lv", [P, V_LAYER], into=region)
            tab = sb("tab", [P, 2, S], into=region)
            tabm = sb("tabm", [P, 2, S], into=region)
            colmask = sb("colmask", [P, GRID], into=region)
            with ExitStack() as r:
                oT = sb("oT", [P, 2, 8, S], F32R, into=r)
                with ExitStack() as r2:
                    pj = sb("pj", [P, 17, S], into=r2)
                    vt = sb("vt", [P, 5, 4, P], into=r2)
                    qst = sb("qst", [P, 2, S], into=r2)
                    kst = sb("kst", [P, S], into=r2)
                    bias = sb("bias", [P, 4, 14, GRID], into=r2)
                    sS, prob = work[:, 2:4, :], sq
                    pT = sb("pT", [P, 2, 4, P], into=r2)
                    osb = sb("osb", [P, 2, P], into=r2)
                    nmax = sb("nmax", [P, 2], into=r2)
                    rsum = sb("rsum", [P, 4], into=r2)
                    rinv = sb("rinv", [P, 4], into=r2)
                with ExitStack() as r2:
                    mg = sb("mg", [P, 2, KD, S], F32R, into=r2)
                    sg = sb("sg", [P, 3, S], into=r2)
            with ExitStack() as r:
                act_f = sb("act_f", [P, 2, KF, S], F32R, into=r)
                tg = sb("tg", [P, 2, S], into=r)
            with ExitStack() as r:
                rows = sb("rows", [DEPTH * 60, 127], into=r)
                cs = sb("cs", [P, 2, D], into=r)
                dots = sb("dots", [P, RING], into=r)
                prod = sb("prod", [P, D], into=r)

        passed = sem("passed")
        with ExitStack() as r:
            mR = sb("mR", [P, 2, KD, S], F32R, into=r)
            with ExitStack() as r2:
                vec2 = sb("vec2", [P, KD, W_M], into=r2)
                half2 = sb("half2", [P, KD, W_M], into=r2)
                lev = sb("lev", [P, LEVELS + 4, P], into=r2)
                k1 = sb("k1", [P, KD], into=r2)
                sp = sb("sp", [P, 8, KD], into=r2)
                xaR = sb("xaR", [P, 2, S], F32R, into=r2)
                xgR = sb("xgR", [P, 2, S], F32R, into=r2)
                uR = sb("uR", [P, 2, S], F32R, into=r2)
                shf = sb("shf", [P, 2, S + 4], into=r2)
                kB, vB, rB, aB, gB, kkB, bnB, yB = (sb(n, [P, S], into=r2) for n in
                                                          ("kB", "vB", "rB", "aB", "gB", "kkB", "bnB", "yB"))
                dB, e1, e2 = (sb(n, [P, CH, P + 1], into=r2) for n in ("dB", "e1", "e2"))
                msum = dB[:].rearrange("p a n -> p (a n)")[:, 0:S]
                mid = sb("mid", [P, CH], into=r2)
                sg2 = sb("sg2", [P, 3, S], into=r2)
                mats = {n: sb("rw_" + n, [P, 2, CH, P], into=r2) for n in ("LT", "T", "TT", "X", "MT", "GB", "GK")}
                vtok, btok, ktok = mats["T"][:, 0], mats["T"][:, 1], mats["X"][:, 0]
                us, sas, state = (work[:, 0, P * n:P * (n + 1)].rearrange("p (h n) -> p h n", h=2) for n in range(3))
        with ExitStack() as r:
            mlpR = sb("mlpR", [P, 2, 16, S], F32R, into=r)
            relu = sb("relu", [P, 2, S], into=r)

        (s_in2, vec2_ready, sp_abs, sp_exp, sp_w, sp_ln, xw_ready, xw_tanh, xin_ready, kk_ready, shifted, u_ready, d_ready,
         e_ready, la_ready, lru_ex, lq_ready, lmul_ready, lru_done, prep_ready, bn_ready, bn_sum, tok_psum, tok_ready,
         mat_ready, mat_used, u_psum, u_sb, sa_psum, sa_sb, st_psum, st_sb, y_psum, y_sb, mean_ready, yc_ready,
         m_done, relu_ready, mlp_ready, xf_ready) = (sem(n) for n in (
            "s_in2", "vec2_ready", "sp_abs", "sp_exp", "sp_w", "sp_ln", "xw_ready", "xw_tanh", "xin_ready", "kk_ready",
            "shifted", "u_ready", "d_ready", "e_ready", "la_ready", "lru_ex", "lq_ready", "lmul_ready", "lru_done",
            "prep_ready", "bn_ready", "bn_sum", "tok_psum", "tok_ready", "mat_ready", "mat_used", "u_psum", "u_sb",
            "sa_psum", "sa_sb", "st_psum", "st_sb", "y_psum", "y_sb", "mean_ready", "yc_ready", "m_done",
            "relu_ready", "mlp_ready", "xf_ready"))
        s_in = sem("s_in")
        s_rows = sem("s_rows")
        s_pad = sem("s_pad")
        s_bias = sem("s_bias")
        bias_ready = sem("bias_ready")
        raw_ready = [sem(f"raw_ready{i}") for i in range(RING)]
        hi_ready = [sem(f"hi_ready{i}") for i in range(RING)]
        tile_ready = sem("tile_ready")
        tile_used = sem("tile_used")
        ada_used = sem("ada_used")
        cs_tanh = sem("cs_tanh")
        s_c = sem("s_c")
        bank_free = [sem("bank_free0"), sem("bank_free1")]
        part_ready = sem("part_ready")
        sq_ready, sq_used = sem("sq_ready"), sem("sq_used")
        root_ready, root_used = sem("root_ready"), sem("root_used")
        h_ready = sem("h_ready")
        lat_ready = sem("lat_ready")
        turned = sem("turned")
        turn_used = sem("turn_used")
        stage_ready = sem("stage_ready")
        scores_ready, max_ready, probs_ready = sem("scores_ready"), sem("max_ready"), sem("probs_ready")
        pv_done, o_used = sem("pv_done"), sem("o_used")
        ot_ready, ot_used = sem("ot_ready"), sem("ot_used")
        kin_ready = sem("kin_ready")
        gate_ready = sem("gate_ready")
        mg_ready = sem("mg_ready")
        up_tanh = sem("up_tanh")
        act_ready = sem("act_ready")
        vec_done, act_done = sem("vec_done"), sem("act_done")
        fin_ready = sem("fin_ready")
        s_out = sem("s_out")

        def evacuated(eng, p):
            eng.wait_ge(bank_free[p.mod(2)], ((p - p.mod(2)).half() + C_BANK + 1).value())

        block = ctx.enter_context(nc.Block())
        N_ADA = DEPTH * NMOD * KD
        GROUPS = T_TOTAL // RING

        @block.sync
        def _(sp):
            sp.dma_start(cs[:, 0, :], c.broadcast_to([P, D])).then_inc(s_c, 16)
            for u in range(RING):
                sp.dma_start(raw[:, u, :], weights[u]).then_inc(raw_ready[u], 16)
            for dst, src in ((adab, ada_b), (vl, vec1), (tab, tables1["axial"]), (vecx, vecx_in), (tabm, tables1["rope"]),
                             (colmask, tables1["colmask"]), (ident, tables1["ident"]), (blk, tables1["blk"]),
                             (xT, x)):
                sp.dma_start(dst[:], src).then_inc(s_in, 16)
            with sp.Fori(1, N_ADA // RING) as i:
                for u in range(RING):
                    sp.wait_ge(ada_used, i * RING + (u - RING + 2))
                    sp.dma_start(raw[:, u, :], weights[bass.ds(i * RING + u, 1)].rearrange("a p n -> (a p) n")
                                 ).then_inc(raw_ready[u], 16)
            for u in range(RING):
                sp.wait_ge(ada_used, N_ADA - RING + 2 + u)
                sp.dma_start(raw[:, u, :], weights[N_ADA + u]).then_inc(raw_ready[u], 16)
            with sp.Fori(1, GROUPS) as i:
                for u in range(RING):
                    sp.wait_ge(tile_ready, i * RING + (u - RING + 1))
                    sp.dma_start(raw[:, u, :], weights[bass.ds(i * RING + (N_ADA + u), 1)].rearrange("a p n -> (a p) n")
                                 ).then_inc(raw_ready[u], 16)
            sp.wait_ge(fin_ready, KD)
            sp.dma_start(out, xT[:]).then_inc(s_out, 16)
            sp.wait_ge(s_out, 16)

        @block.gpsimd
        def _(pool):
            def cast(i, u, fresh):
                pool.wait_ge(raw_ready[u], (i + (N_ADA // RING + 1)) * 16)
                if not fresh:
                    pool.wait_ge(tile_used, i * RING + (u - RING + 1))
                pool.sem_inc(passed, 1)
                pool.dma_start(wR[:, u, 0, :], raw[:, u, :]).then_inc(hi_ready[u], 16)

            def group(i, first, last):
                for u in range(RING):
                    if u < RING - AHEAD:
                        cast(i, u + AHEAD, first)
                    elif not last:
                        cast(i + 1, u + AHEAD - RING, False)
                    pool.wait_ge(hi_ready[u], (i + 1) * 16)
                    nc.gpsimd.tensor_tensor(wR[:, u, 1, :], raw[:, u, :], wR[:, u, 0, :], ALU.subtract
                                            ).then_inc(tile_ready, 1)

            for u in range(AHEAD):
                cast(0, u, True)
            group(0, True, False)
            with pool.Fori(1, GROUPS - 1) as i:
                group(i, False, False)
            group(GROUPS - 1, False, True)

        @block.scalar
        def _(act):
            A = nc.scalar.activation
            done = Steps(act, act_done, {}, passed)
            act.wait_ge(s_pad, 1)
            act.dma_start(rows[:, 48:79], rpb).then_inc(s_rows, 16)
            act.wait_ge(s_rows, 16)
            act.dma_start(dram_bias.ap(), rows[:]).then_inc(s_rows, 16)
            act.wait_ge(s_c, 16)
            A(cs[:, 1, :], cs[:, 0, :], ACT.Tanh, scale=0.5).then_inc(cs_tanh, 1)
            act.wait_ge(s_in, 16 * 9)
            act.wait_ge(s_rows, 32)
            for lh in range(DEPTH * 4):
                act.dma_start(bass.AP(dram_toeplitz, GRID * 15 * SKEW * lh, [[SKEW, 15], [15 * SKEW + 1, GRID], [1, 127]]),
                              bass.AP(dram_bias, 127 * 15 * lh, [[127, 15], [0, GRID], [1, 127]])).then_inc(s_rows, 16)
            act.wait_ge(s_rows, 32 + 16 * DEPTH * 4)

            def square(src, q):
                act.wait_ge(sq_used, (q + (1 - 2 + C_UNIT)).value())
                A(sq[:, q.mod(2), :], src, ACT.Square).then_inc(sq_ready, 1)

            def root(q, r, width, eps=0):
                act.wait_ge(sq_used, (q + (1 + C_UNIT)).value())
                act.wait_ge(root_used, (r + 1).value())
                A(rt, ps[:, SUM, :], ACT.Sqrt, bias=epsb[:, eps:eps + 1], scale=1.0 / width).then_inc(root_ready, 1)

            def norm(q, r, p):
                for k in range(KD):
                    evacuated(act, p + k)
                    square(xT[:, k, :], q + k)
                root(q + (KD - 1), r, D)

            act.wait_ge(s_pad, 2)
            act.wait_ge(vec_done, 3)
            with done.loop("layer", DEPTH) as l:
                Q, R, PR, TI = Count(0).at(l, 24), Count(0).at(l, 9), Count(0).at(l, P_LAYER), Count(0).at(l, T_LAYER)
                norm(Q, R, PR - KD)
                for half in range(2):
                    for h in range(4):
                        src = dram_toeplitz.ap()[bass.ds(l * 4 + h, 1), :, 1 - half:15 - half, GRID - 1:127]
                        act.dma_start(bias[64 * half:64 * half + 64, h],
                                      src.rearrange("a p j n -> (a p) j n")).then_inc(s_bias, 16)
                with done.loop("in", 4) as i:
                    for u in range(4):
                        act.wait_ge(tile_used, (TI + (T_IN + u + 1)).at(i, 4).value())
                        A(pj[:, bass.ds(i * 4 + u, 1), :].rearrange("p a n -> p (a n)"), ps[:, ACC + u % 2, :],
                          ACT.Copy).then_inc(bank_free[u % 2], 1)
                q, r = Q + KD, R + 1
                for tiles, width in (((6, 7), 256), ((8,), 128), ((10,), 64), ((11,), 64), ((12,), 64), ((13,), 64), ((14,), 64)):
                    for t in tiles:
                        evacuated(act, PR + t)
                        square(pj[:, t, :], q)
                        q = q + 1
                    root(q - 1, r, width)
                    r = r + 1
                TU = Count(0).at(l, 69)

                def turn(j, t):
                    act.wait_ge(turned, (j + 1).value())
                    A(vt[:, t].rearrange("p a n -> p (a n)"), ps[:, PT + t % 2, :], ACT.Copy).then_inc(turn_used, 1)

                for j, t in enumerate((0, 1, 4)):
                    turn(TU + j, t)

                def pair(U, J, masked):
                    for s in range(9):
                        if s < 8:
                            act.wait_ge(max_ready, (U + (s + 1)).value())
                            act.wait_ge(o_used, (U + (s + 1)).value())
                            act.wait_ge(turned, (J + s - 1).value()) if s >= 2 else None
                            A(prob[:, s % 2, :], sS[:, s % 2, :] if masked else ps[:, SC + s % 2, :], ACT.Exp,
                              bias=nmax[:, s % 2:s % 2 + 1], accum_out=rsum[:, s % 4:s % 4 + 1]).then_inc(probs_ready, 1)
                        if s >= 1:
                            u = s - 1
                            act.wait_ge(turned, (J + (u + 1)).value())
                            act.wait_ge(pv_done, (U + (u - 1 + C_UNIT)).value())
                            A(pT[:, u % 2].rearrange("p a n -> p (a n)"), ps[:, PT + u % 2, :], ACT.Copy).then_inc(turn_used, 1)

                with done.loop("na", 2) as i:
                    pair(Count(0).at(l, 64).at(i, 8), (TU + 3).at(i, 8), True)
                for h in range(4):
                    p = PR + (P_MLA + h)
                    act.wait_ge(*((part_ready, (Count(h // 2 + 1).at(l, 22)).value()) if h % 2 == 0 else
                                  (tile_used, (TI + (T_MLA + h // 2 + 1)).value())))
                    A(pj[0:96, h, :], ps[0:96, ACC + h % 2, :], ACT.Copy).then_inc(bank_free[h % 2], 1)
                for h in range(4):
                    act.wait_ge(*((part_ready, (Count(3 + h).at(l, 22)).value()) if h < 3 else
                                  (tile_used, (TI + (T_MLA + 3)).value())))
                    A(pj[0:64, 4 + h, :], ps[0:64, ACC + h % 2, :], ACT.Copy).then_inc(bank_free[h % 2], 1)
                for h in range(2):
                    act.wait_ge(*((part_ready, (Count(6).at(l, 22)).value()) if h < 1 else
                                  (tile_used, (TI + (T_MLA + 4)).value())))
                    A(pj[:, (8, 16)[h], :], ps[:, ACC + h % 2, :], ACT.Copy).then_inc(bank_free[h % 2], 1)
                for j, t in enumerate((2, 3)):
                    turn(TU + (19 + j), t)
                with done.loop("mla", 2) as i:
                    pair(Count(16).at(l, 64).at(i, 8), (TU + 21).at(i, 8), False)
                with done.loop("gqa", 4) as i:
                    pair(Count(32).at(l, 64).at(i, 8), (TU + 37).at(i, 8), False)
                with done.loop("merge", KD) as m:
                    act.wait_ge(mg_ready, Count(1).at(l, KD).at(m, 1).value())
                    for g in range(3):
                        act.wait_ge(tile_used, (TI + (T_MERGE + g + 1)).at(m, 4).value())
                        A(sg[:, g, :], ps[:, ACC + g % 2, :], ACT.Tanh, scale=0.5).then_inc(bank_free[g % 2], 1)
                norm(Q + 16, R + 8, PR + P_OUT)
                with done.loop("gu", KF // 2) as i:
                    for j in range(2):
                        act.wait_ge(act_ready, Count(j - 2 + C_UNIT + 1).at(l, KF).at(i, 2).value())
                        act.wait_ge(tile_used, (TI + (T_GU + 2 * j + 1)).at(i, 4).value())
                        A(tg[:, j, :], ps[:, ACC, :], ACT.Tanh, scale=0.5).then_inc(up_tanh, 1)
            Q0, R0 = 24 * DEPTH + KD, 9 * DEPTH + 1
            norm(Count(Q0 - KD), Count(R0 - 1), Count(P_B2 - KD))
            for k in range(KD):
                act.wait_ge(xf_ready, k + 1)
                square(xT[:, k, :], Count(Q0 + k))
            root(Count(Q0 + KD - 1), Count(R0), D)
            for dst, src in ((vec2, vec2_in), (lev, tables1["levels"])):
                act.dma_start(dst[:], src).then_inc(s_in2, 16)
            act.wait_ge(sp_abs, 1)
            A(sp[:, 1, :], sp[:, 0, :], ACT.Exp, scale=-1.0).then_inc(sp_exp, 1)
            act.wait_ge(sp_w, 1)
            A(sp[:, 3, :], sp[:, 2, :], ACT.Ln).then_inc(sp_ln, 1)

            def bank_to(dst, p, t=None, func=ACT.Copy, **kw):
                if t is not None:
                    act.wait_ge(tile_used, (t + 1).value())
                A(dst, ps[:, ACC + p.mod(2), :], func, **kw).then_inc(bank_free[p.mod(2)], 1)

            for j in range(2):
                bank_to(shf[:, j, 3:S + 3], Count(P_B2 + j), Count(T_B2 + j))
            act.wait_ge(xw_ready, 1)
            A(kB[0:64, :], kB[0:64, :], ACT.Tanh).then_inc(xw_tanh, 1)
            act.wait_ge(xw_ready, 2)
            A(vB[:], vB[:], ACT.Tanh, scale=0.5).then_inc(xw_tanh, 1)
            act.wait_ge(xin_ready, 2)
            act.wait_ge(vec2_ready, 1)
            with done.loop("m", KD) as m:
                Pm, Tm = Count(P_B2 + 2).at(m, P_M), Count(T_B2 + 2).at(m, T_M)
                PARTS0 = 22 * DEPTH

                def part(n):
                    act.wait_ge(part_ready, Count(PARTS0 + n).at(m, 4).value())

                def vec(table, col):
                    return table[:, bass.ds(m, 1), col:col + 1].rearrange("p a n -> p (a n)")

                for j in range(4):
                    act.wait_ge(shifted, Count((2, 2, 3, 4)[j]).at(m, 5).value())
                    bank_to(shf[:, j % 2, 3:S + 3], Pm + j, Tm + j)
                    if j == 2:
                        act.wait_ge(kk_ready, Count(1).at(m, 1).value())
                        square(kkB[:], Count(Q0 + 8).at(m, 2))
                act.wait_ge(m_done, Count(1).at(m, 1).value())
                part(1)
                bank_to(e1[:, :, 0:P], Pm + 4, func=ACT.Tanh, bias=vec(half2, W_W0), scale=0.5)
                part(2)
                bank_to(aB[:], Pm + 5, func=ACT.Tanh, bias=vec(half2, W_A0), scale=0.5)
                part(3)
                bank_to(gB[:], Pm + 6)
                root(Count(Q0 + 8).at(m, 2), Count(R0 + 1).at(m, 2), 1, 1)
                act.wait_ge(d_ready, Count(1).at(m, 1).value())
                A(e1[:], dB[:], ACT.Exp, scale=-1.0).then_inc(e_ready, 1)
                A(e2[:], dB[:], ACT.Exp).then_inc(e_ready, 1)
                part(4)
                bank_to(sg2[:, 0, :], Pm + 7, func=ACT.Tanh, bias=vec(half2, W_BA), scale=0.5)
                bank_to(sg2[:, 1, :], Pm + 8, Tm + T_SMALL, func=ACT.Tanh, bias=vec(half2, W_BI), scale=0.5)
                act.wait_ge(la_ready, Count(1).at(m, 1).value())
                A(sg2[:, 2, :], sg2[:, 0, :], ACT.Exp).then_inc(lru_ex, 1)
                A(yB[:], sg2[:, 0, :], ACT.Tanh, scale=-1.0).then_inc(lru_ex, 1)
                bank_to(msum, Pm + 9, Tm + 5)
                act.wait_ge(lq_ready, Count(1).at(m, 1).value())
                A(yB[:], yB[:], ACT.Sqrt).then_inc(lmul_ready, 1)
                act.wait_ge(lru_done, Count(1).at(m, 1).value())
                bank_to(yB[:], Pm + 12, Tm + 8, func=ACT.Gelu_apprx_tanh)
                for g in range(3):
                    if g < 3:
                        bank_to(sg2[:, g, :], Pm + (13 + g), Tm + (9 + g), func=ACT.Tanh, bias=vec(half2, W_MB + g), scale=0.5)
                for j, dst in enumerate((vtok, btok, ktok)):
                    act.wait_ge(tok_psum, Count(j + 1).at(m, 3).value())
                    A(dst.rearrange("p a n -> p (a n)"), ps[:, 6 + j % 2, :], ACT.Copy).then_inc(tok_ready, 1)
                for c_ in range(CH):
                    for h in range(2):
                        act.wait_ge(u_psum, Count(2 * c_ + h + 1).at(m, 8).value())
                        A(us[:, h, :], ps[:, 2 + h, 0:64], ACT.Copy).then_inc(u_sb, 1)
                    for h in range(2):
                        act.wait_ge(sa_psum, Count(2 * c_ + h + 1).at(m, 8).value())
                        A(sas[:, h, :], ps[:, 4 + h, 0:64], ACT.Copy).then_inc(sa_sb, 1)
                act.wait_ge(y_psum, Count(1).at(m, 1).value())
                A(yB[:], ps[:, 6, :], ACT.Copy).then_inc(y_sb, 1)
                act.wait_ge(yc_ready, Count(1).at(m, 1).value())
                square(yB[:], Count(Q0 + 9).at(m, 2))
                root(Count(Q0 + 9).at(m, 2), Count(R0 + 2).at(m, 2), 64, 2)
            Q1, R1 = Q0 + 8 + 2 * KD, R0 + 1 + 2 * KD
            norm(Count(Q1), Count(R1), Count(P_OUT2))
            with done.loop("mlp", 2) as hh:
                with done.loop("mlp1", 4) as i:
                    for u in range(4):
                        act.wait_ge(mlp_ready, Count(u - 2 + C_UNIT + 1).at(hh, 16).at(i, 4).value())
                        act.wait_ge(tile_used, Count(T_MLP + u + 1).at(hh, 32).at(i, 4).value())
                        A(relu[:, u % 2, :], ps[:, ACC + u % 2, :], ACT.Relu).then_inc(relu_ready, 1)
            norm(Count(Q1 + KD), Count(R1 + 1), Count(P_MLP + 24 * 2 - KD))

        @block.tensor
        def _(pe):
            MM = nc.tensor.matmul
            def claim(p):
                b = p.mod(2)
                pe.wait_ge(bank_free[b], ((p - b).half() + C_BANK).value())
                return ACC + b

            def weight(slot, part, col, width=P, rows=P):
                return wR[0:rows, slot, part, col:col + width]

            def need_tile(t):
                pe.wait_ge(tile_ready, (t + 1).value())
                return t.mod(RING)

            def product(t, p, r_hi, r_lo, h_from=None):
                slot, bank = need_tile(t), claim(p)
                for k in range(KD):
                    if h_from is not None:
                        pe.wait_ge(h_ready, (h_from + (k + 1)).value())
                    mm = three_passes(MM, ps[:, bank, :], weight(slot, 0, k * P), weight(slot, 1, k * P),
                                      r_hi(k), r_lo(k), k == 0, k == KD - 1)
                mm.then_inc(tile_used, 1)

            def h_hi(k):
                return hR[:, 0, k, :]

            def h_lo(k):
                return hR[:, 1, k, :]

            def sum_squares(q, r, n, ones_):
                pe.wait_ge(root_used, (r + 1).value())
                for k in range(n):
                    pe.wait_ge(sq_ready, (q + (k + 1)).value())
                    MM(ps[:, SUM, :], ones_[:], sq[:, (q + k).mod(2), :], start=(k == 0), stop=(k == n - 1)
                       ).then_inc(sq_used, 1)

            pe.sem_inc(passed, 1)
            with pe.Fori(0, DEPTH) as l:
                Q, R, PR, TI = Count(0).at(l, 24), Count(0).at(l, 9), Count(0).at(l, P_LAYER), Count(0).at(l, T_LAYER)
                H = Count(0).at(l, 2 * KD)
                TU = Count(0).at(l, 69)
                sum_squares(Q, R, KD, ones)
                pe.sem_inc(passed, 1)
                with pe.Fori(0, 4) as i:
                    for u in range(4):
                        product((TI + (T_IN + u)).at(i, 4), (PR + (P_IN + u)).at(i, 4), h_hi, h_lo, H if u == 0 else None)
                q, r = Q + KD, R + 1
                for n, o in ((2, ones), (1, ones)) + ((1, blk),) * 5:
                    sum_squares(q, r, n, o)
                    q, r = q + n, r + 1

                def turn(j, t, tile, p):
                    evacuated(pe, PR + p)
                    pe.wait_ge(turn_used, (j + 1).value())
                    for b in range(4):
                        mm = nc.tensor.transpose(ps[:, PT + t % 2, b * P:(b + 1) * P], pj[:, tile, b * P:(b + 1) * P], ident[:])
                    mm.then_inc(turned, 1)

                for j, (t, tile) in enumerate(((0, 4), (1, 5), (4, 15))):
                    turn(TU + j, t, tile, tile)

                def pair(U, J, n_pair, rows_q, rhs_k, tile_v):
                    pe.wait_ge(stage_ready, (n_pair + 1).value())
                    B = U.half()
                    for s in range(11):
                        if s < 8:
                            b, h = s // 2, s % 2
                            pe.wait_ge(probs_ready, (U + (s - 1 + C_UNIT)).value())
                            MM(ps[:, SC + s % 2, :], rows_q(h, b), rhs_k(h), start=True, stop=True).then_inc(scores_ready, 1)
                        if 1 <= s < 9:
                            u = s - 1
                            pe.wait_ge(probs_ready, (U + (u + 1 + C_UNIT)).value())
                            pe.wait_ge(turn_used, (J + (u + 1 if u == 0 else u)).value())
                            for kb in range(4):
                                mm = nc.tensor.transpose(ps[:, PT + u % 2, kb * P:(kb + 1) * P],
                                                         prob[:, u % 2, kb * P:(kb + 1) * P], ident[:])
                            mm.then_inc(turned, 1)
                        if 2 <= s < 10:
                            u = s - 2
                            pe.wait_ge(turn_used, (J + (u + 1 + 1)).value())
                            pe.wait_ge(o_used, (U + (u + 3)).value())
                            for kb in range(4):
                                mm = MM(ps[:, OB + u % 2, 0:64], pT[:, u % 2, kb, :],
                                        tile_v(kb, u % 2), start=(kb == 0), stop=(kb == 3))
                            mm.then_inc(pv_done, 1)
                        if s >= 4 and s % 2 == 0:
                            b = s // 2 - 2
                            pe.wait_ge(o_used, (U + (2 * b + 2 + 4)).value())
                            pe.wait_ge(ot_used, (B + (b - 1 + C_UNIT)).value())
                            nc.tensor.transpose(ps[:, ACC + b % 2, 0:P], osb[:, b % 2, :], ident[:]
                                                ).then_inc(ot_ready, 1)

                def v_of(t, *at):
                    return lambda kb, h: vt[:, t(at), kb, 64 * h:64 * h + 64]

                pe.sem_inc(passed, 1)
                with pe.Fori(0, 2) as i:
                    pair(Count(0).at(l, 64).at(i, 8), (TU + 3).at(i, 8), Count(0).at(l, 8).at(i, 1),
                         lambda h, b: qst[64 * h:64 * h + 64, 0, b * P:(b + 1) * P],
                         lambda h: kst[64 * h:64 * h + 64, :],
                         lambda kb, h: vt[:, bass.ds(i, 1), kb, 64 * h:64 * h + 64].rearrange("p a n -> p (a n)"))
                pe.wait_ge(lat_ready, Count(3).at(l, 3).value())
                pe.wait_ge(ot_used, Count(8 + C_UNIT).at(l, 32).value())
                for h in range(4):
                    slot, bank = need_tile(TI + (T_MLA + h // 2)), claim(PR + (P_MLA + h))
                    for k in range(2):
                        col = k * 192 + (h % 2) * 96
                        mm = three_passes(MM, ps[0:96, bank, :], weight(slot, 0, col, 96), weight(slot, 1, col, 96),
                                          oT[:, 0, 4 + k, :], oT[:, 1, 4 + k, :], k == 0, k == 1)
                    mm.then_inc(tile_used if h % 2 else part_ready, 1)
                for h in range(4):
                    slot, bank = need_tile(TI + (T_MLA + 2)), claim(PR + (P_MLA + 4 + h))
                    mm = three_passes(MM, ps[0:64, bank, :], weight(slot, 0, h * 64, 64), weight(slot, 1, h * 64, 64),
                                      oT[:, 0, 6, :], oT[:, 1, 6, :], True, True)
                    mm.then_inc(tile_used if h == 3 else part_ready, 1)
                for h in range(2):
                    slot, bank = need_tile(TI + (T_MLA + 3)), claim(PR + (P_MLA + 8 + h))
                    mm = three_passes(MM, ps[:, bank, :], weight(slot, 0, h * P), weight(slot, 1, h * P),
                                      oT[:, 0, 6, :], oT[:, 1, 6, :], True, True)
                    mm.then_inc(tile_used if h == 1 else part_ready, 1)
                turn(TU + 19, 2, 8, P_MLA + 8)
                turn(TU + 20, 3, 16, P_MLA + 9)
                pe.sem_inc(passed, 1)
                with pe.Fori(0, 2) as i:
                    pair(Count(16).at(l, 64).at(i, 8), (TU + 21).at(i, 8), Count(2).at(l, 8).at(i, 1),
                         lambda h, b: qst[0:96, h, b * P:(b + 1) * P],
                         lambda h: pj[0:96, bass.ds(i * 2 + (4 + h), 1), :].rearrange("p a n -> p (a n)"),
                         lambda kb, h: vt[:, bass.ds(i + 2, 1), kb, 64 * h:64 * h + 64].rearrange("p a n -> p (a n)"))
                pe.sem_inc(passed, 1)
                with pe.Fori(0, 4) as i:
                    pair(Count(32).at(l, 64).at(i, 8), (TU + 37).at(i, 8), Count(4).at(l, 8).at(i, 1),
                         lambda h, b: qst[64 * h:64 * h + 64, 0, b * P:(b + 1) * P],
                         lambda h: pj[64 * h:64 * h + 64, 14, :],
                         lambda kb, h: vt[:, 4, kb, 64 * h:64 * h + 64])
                pe.wait_ge(ot_used, Count(32 + C_UNIT).at(l, 32).value())
                pe.sem_inc(passed, 1)
                with pe.Fori(0, KD) as m:
                    T, PP = (TI + T_MERGE).at(m, 4), (PR + P_MERGE).at(m, 6)
                    for g in range(3):
                        product(T + g, PP + g, h_hi, h_lo)
                    slot = need_tile(T + 3)
                    for g, ks in enumerate(((0, 1), (2, 3), (4, 5, 6, 7))):
                        bank = claim(PP + (3 + g))
                        for k in ks:
                            mm = three_passes(MM, ps[:, bank, :], weight(slot, 0, k * P), weight(slot, 1, k * P),
                                              oT[:, 0, k, :], oT[:, 1, k, :], k == ks[0], k == ks[-1])
                        mm.then_inc(tile_used if g == 2 else part_ready, 1)
                pe.wait_ge(mg_ready, Count(KD + 1).at(l, KD).value())
                pe.sem_inc(passed, 1)
                with pe.Fori(0, 2) as i:
                    for u in range(4):
                        product((TI + (T_OUT + u)).at(i, 4), (PR + (P_OUT + u)).at(i, 4),
                                lambda k: mg[:, 0, k, :], lambda k: mg[:, 1, k, :])
                sum_squares(Q + 16, R + 8, KD, ones)
                pe.sem_inc(passed, 1)
                with pe.Fori(0, KF // 2) as i:
                    for u in range(4):
                        product((TI + (T_GU + u)).at(i, 4), (PR + (P_GU + u)).at(i, 4), h_hi, h_lo, H + KD if u == 0 else None)
                pe.wait_ge(act_ready, Count(KF + C_UNIT).at(l, KF).value())
                pe.sem_inc(passed, 1)
                with pe.Fori(0, 2) as i:
                    for u in range(4):
                        bank = claim((PR + (P_DOWN + u)).at(i, 4))
                        for t in range(3):
                            slot = need_tile((TI + (T_DOWN + 3 * u + t)).at(i, 12))
                            for k in range(8 * t, min(8 * t + 8, KF)):
                                col = (k - 8 * t) * P
                                mm = three_passes(MM, ps[:, bank, :], weight(slot, 0, col), weight(slot, 1, col),
                                                  act_f[:, 0, k, :], act_f[:, 1, k, :], k == 0, k == KF - 1)
                            mm.then_inc(tile_used, 1)
            Q0, R0, H0 = 24 * DEPTH + KD, 9 * DEPTH + 1, 2 * KD * DEPTH
            sum_squares(Count(Q0 - KD), Count(R0 - 1), KD, ones)
            sum_squares(Count(Q0), Count(R0), KD, ones)
            for j in range(2):
                product(Count(T_B2 + j), Count(P_B2 + j), h_hi, h_lo, Count(H0) if j == 0 else None)
            pe.wait_ge(xin_ready, 2)
            pe.sem_inc(passed, 1)
            with pe.Fori(0, KD) as m:
                Pm, Tm = Count(P_B2 + 2).at(m, P_M), Count(T_B2 + 2).at(m, T_M)
                for j in range(4):
                    product(Tm + j, Pm + j, h_hi, h_lo)
                slot = need_tile(Tm + T_SMALL)
                for j, (lo_, hi_, col, src) in enumerate(((0, 64, 0, xaR), (64, P, 0, xaR), (0, P, 1, xgR), (0, P, 2, uR), (0, P, 3, uR))):
                    bank = claim(Pm + (4 + j))
                    if j == 3:
                        pe.wait_ge(u_ready, Count(1).at(m, 1).value())
                    w = [wR[lo_:hi_, slot, part, col * P:(col + 1) * P] for part in range(2)]
                    mm = three_passes(MM, ps[:, bank, :], w[0], w[1], src[lo_:hi_, 0, :], src[lo_:hi_, 1, :], True, True)
                    mm.then_inc(part_ready if j < 4 else tile_used, 1)
                sum_squares(Count(Q0 + 8).at(m, 2), Count(R0 + 1).at(m, 2), 1, blk)
                for j in range(7):
                    product(Tm + (5 + j), Pm + (9 + j), h_hi, h_lo)
                pe.wait_ge(prep_ready, Count(1).at(m, 1).value())
                ops = {"LT": (aB, kkB), "L": (kkB, aB), "GB": (aB, rB), "MT": (kB, kkB), "GK": (kB, rB)}

                def used(kind, h, lv=0):
                    pe.wait_ge(mat_used, Count(RW.index((kind, h, lv)) + 1).at(m, len(RW)).value())

                for kind, h, lv in RW:
                    bank = RW_BANK[kind] + h
                    if kind == "MT":
                        used("LT", h)
                    if kind == "GK":
                        used("L", h)
                    if kind == "X":
                        used("TT", h, lv - 1) if lv > 1 else used("MT", h)
                    if kind in ("T", "TT"):
                        used("X", h, lv)
                        if lv == 1:
                            used("GK", h)
                    for cc in range(CH):
                        cols = slice(cc * P, (cc + 1) * P)
                        if lv == 0:
                            a_, b_ = ops[kind]
                            lhs, rhs = a_[64 * h:64 * h + 64, cols], b_[64 * h:64 * h + 64, cols]
                        else:
                            a_, b_ = {"X": ("LT", "T"), "T": ("TT", "X"), "TT": ("X", "TT")}[kind]
                            lhs, rhs = mats[a_][:, h, cc, :], mats[b_][:, h, cc, :]
                        mm = MM(ps[:, bank, cols], lhs, rhs, start=True, stop=True)
                    mm.then_inc(mat_ready, 1)
                for h in range(2):
                    used("TT", h, LEVELS)
                for j, src in enumerate((vB, aB, kB)):
                    if j == 2:
                        pe.wait_ge(tok_ready, Count(1).at(m, 3).value())
                    for cc in range(CH):
                        mm = nc.tensor.transpose(ps[:, 6 + j % 2, cc * P:(cc + 1) * P], src[:, cc * P:(cc + 1) * P], ident[:])
                    mm.then_inc(tok_psum, 1)
                pe.wait_ge(tok_ready, Count(3).at(m, 3).value())
                for cc in range(CH):
                    n = 2 * cc
                    old, cols = state[:, cc % 2, :], slice(cc * P, (cc + 1) * P)
                    for h in range(2):
                        rows_ = slice(64 * h, 64 * h + 64)
                        if cc:
                            pe.wait_ge(st_sb, Count(2 * (cc - 1) + h + 1).at(m, 6).value())
                            MM(ps[:, 2 + h, 0:64], kkB[rows_, cols], old[rows_, :], start=True, stop=False)
                        MM(ps[:, 2 + h, 0:64], mats["MT"][:, h, cc, :], vtok[:, cc, rows_], start=not cc, stop=True).then_inc(u_psum, 1)
                    for h in range(2):
                        pe.wait_ge(u_sb, Count(n + h + 1).at(m, 8).value())
                        MM(ps[:, 4 + h, 0:64], mats["TT"][:, h, cc, :], us[:, h, :], start=True, stop=True).then_inc(sa_psum, 1)
                    for h in range(2):
                        rows_ = slice(64 * h, 64 * h + 64)
                        pe.wait_ge(sa_sb, Count(n + h + 1).at(m, 8).value())
                        if cc < CH - 1:
                            MM(ps[rows_, 7, 0:64], btok[:, cc, rows_], sas[:, h, :], start=True, stop=False)
                            MM(ps[rows_, 7, 0:64], ktok[:, cc, rows_], vtok[:, cc, rows_], start=False, stop=True).then_inc(st_psum, 1)
                    for h in range(2):
                        rows_ = slice(64 * h, 64 * h + 64)
                        MM(ps[rows_, 6, cols], sas[:, h, :], mats["GB"][:, h, cc, :], start=True, stop=False)
                        if cc:
                            MM(ps[rows_, 6, cols], old[rows_, :], rB[rows_, cols], start=False, stop=False)
                        mm = MM(ps[rows_, 6, cols], vtok[:, cc, rows_], mats["GK"][:, h, cc, :], start=False, stop=True)
                mm.then_inc(y_psum, 1)
                MM(ps[:, 3, :], blk[:], bnB[:], start=True, stop=True).then_inc(bn_sum, 1)
                pe.wait_ge(y_sb, Count(1).at(m, 1).value())
                MM(ps[:, 2, :], blk[:], yB[:], start=True, stop=True).then_inc(mean_ready, 1)
                sum_squares(Count(Q0 + 9).at(m, 2), Count(R0 + 2).at(m, 2), 1, blk)
            pe.wait_ge(m_done, KD + 1)
            for u in range(KD):
                product(Count(T_OUT2 + u), Count(P_OUT2 + u), lambda k: mR[:, 0, k, :], lambda k: mR[:, 1, k, :])
            Q1, R1 = Q0 + 8 + 2 * KD, R0 + 1 + 2 * KD
            sum_squares(Count(Q1), Count(R1), KD, ones)
            with pe.Fori(0, 2) as hh:
                with pe.Fori(0, 4) as i:
                    for u in range(4):
                        product(Count(T_MLP + u).at(hh, 32).at(i, 4), Count(P_MLP + u).at(hh, 24).at(i, 4), h_hi, h_lo,
                                Count(H0 + KD) if u == 0 else None)
                pe.wait_ge(mlp_ready, Count(16 + C_UNIT).at(hh, 16).value())
                pe.sem_inc(passed, 1)
                with pe.Fori(0, 4) as i:
                    for u in range(2):
                        bank = claim(Count(P_MLP + 16 + u).at(hh, 24).at(i, 2))
                        for t in range(2):
                            slot = need_tile(Count(T_MLP + 16 + 2 * u + t).at(hh, 32).at(i, 4))
                            for k in range(8):
                                mm = three_passes(MM, ps[:, bank, :], weight(slot, 0, k * P), weight(slot, 1, k * P),
                                                  mlpR[:, 0, 8 * t + k, :], mlpR[:, 1, 8 * t + k, :], t + k == 0, t * 8 + k == 15)
                            mm.then_inc(tile_used, 1)
            sum_squares(Count(Q1 + KD), Count(R1 + 1), KD, ones)

        @block.vector
        def _(dve):
            V = nc.vector
            v = Steps(dve, vec_done, STEPS, passed)
            for b in range(2):
                dve.sem_inc(bank_free[b], C_BANK)
            dve.sem_inc(sq_used, C_UNIT)
            dve.sem_inc(root_used, 1)
            dve.sem_inc(turn_used, 1)
            dve.sem_inc(ada_used, 1)
            dve.sem_inc(probs_ready, C_UNIT)
            dve.sem_inc(pv_done, C_UNIT)
            dve.sem_inc(ot_used, C_UNIT)
            dve.sem_inc(o_used, 4)
            dve.sem_inc(mg_ready, 1)
            dve.sem_inc(act_ready, C_UNIT)
            V.memset(rows[:], 0.0).then_inc(s_pad, 1)
            v(V.memset(ones[:], 1.0))
            for j, e in enumerate((EPS, 0.0, LNX_EPS)):
                ins = V.memset(epsb[:, j:j + 1], e)
                if j < 2:
                    v(ins)
                else:
                    ins.then_inc(s_pad, 1)
            dve.wait_ge(cs_tanh, 1)
            v(V.tensor_scalar(cs[:, 1, :], cs[:, 1, :], 1.0, 0.5, ALU.add, ALU.mult))
            v.sync()
            v(V.tensor_tensor(cs[:, 0, :], cs[:, 0, :], cs[:, 1, :], ALU.mult))
            v.sync()
            with v.loop("mod", N_ADA // RING) as i:
                for u in range(RING):
                    dve.wait_ge(raw_ready[u], i * 16 + 16)
                    dve.wait_ge(ada_used, i * RING + (u + 1))
                    dve.sem_inc(passed, 1)
                    V.tensor_tensor_reduce(prod[:], raw[:, u, :], cs[:, 0, :], 1.0, 0.0, ALU.mult, ALU.add,
                                           accum_out=dots[:, u:u + 1]).then_inc(ada_used, 1)
                dve.wait_ge(ada_used, i * RING + (RING + 1))
                dve.sem_inc(passed, 1)
                v(V.tensor_copy(mod[:, bass.ds(i * RING, RING)], dots[:]))
                v.sync()
            dve.wait_ge(s_in, 16 * 9)
            v(V.tensor_tensor(mod[:], mod[:], adab[:], ALU.add))
            v.sync()

            def take_root(r):
                dve.wait_ge(root_ready, (r + 1).value())
                V.reciprocal(rs, rt).then_inc(root_used, 1)
                dve.wait_ge(root_used, (r + 2).value())

            def split(hi, lo, full, signal, n=1):
                v(V.tensor_copy(hi, full))
                v.sync()
                V.tensor_tensor(lo, full, hi, ALU.subtract).then_inc(signal, n)

            def norm(r, H, scale, shift):
                take_root(r)
                for k in range(KD):
                    v(V.tensor_tensor(tmp, xT[:, k, :], rs, ALU.mult))
                    v.sync()
                    if k:
                        dve.wait_ge(h_ready, (H + k).value())
                    v(V.tensor_scalar(hf, tmp, gs[:, scale, k:k + 1], lm[:, shift + k:shift + k + 1], ALU.mult, ALU.add))
                    v.sync()
                    split(hR[:, 0, k, :], hR[:, 1, k, :], hf, h_ready)

            def residual(t, p, m, gate):
                dve.wait_ge(tile_used, (t + 1).value())
                xm = xT[:, bass.ds(m, 1), :].rearrange("p a n -> p (a n)")
                V.scalar_tensor_tensor(xm, ps[:, ACC + p.mod(2), :], lm[:, bass.ds(m + gate, 1)], xm, ALU.mult, ALU.add
                                       ).then_inc(bank_free[p.mod(2)], 1)

            with v.loop("layer", DEPTH) as l:
                R, PR, TI = Count(0).at(l, 9), Count(0).at(l, P_LAYER), Count(0).at(l, T_LAYER)
                H = Count(0).at(l, 2 * KD)
                TU = Count(0).at(l, 69)
                v(V.tensor_copy(lm[:], mod[:, bass.ds(l * (NMOD * KD), NMOD * KD)]))
                v(V.tensor_copy(lvec[:], vl[:, bass.ds(l * V_LAYER, V_LAYER)]))
                v.sync()
                v(V.scalar_tensor_tensor(gs[:, 0, :], lm[:, SC_M:SC_M + KD], 1.0, lvec[:, V_MIX:V_MIX + KD], ALU.add, ALU.mult))
                v(V.scalar_tensor_tensor(gs[:, 1, :], lm[:, SC_F:SC_F + KD], 1.0, lvec[:, V_FFN:V_FFN + KD], ALU.add, ALU.mult))
                v.sync()
                norm(R, H, 0, SH_M)
                dve.wait_ge(s_bias, Count(128).at(l, 128).value())
                bv = bias[:].rearrange("p h j n -> p (h j) n")
                V.tensor_tensor(bv, bv, colmask[:].unsqueeze(1).broadcast_to([P, 56, GRID]), ALU.add).then_inc(bias_ready, 1)
                r = R + 1
                for tiles, gain, dst in (((6, 7), V_CQ, 4), ((8,), V_CKV, 6)):
                    take_root(r)
                    r = r + 1
                    for n, t in enumerate(tiles):
                        evacuated(dve, PR + t)
                        v(V.scalar_tensor_tensor(tmp, pj[:, t, :], lvec[:, gain + n:gain + n + 1], rs, ALU.mult, ALU.mult))
                        v.sync()
                        split(oT[:, 0, dst + n, :], oT[:, 1, dst + n, :], tmp, lat_ready)
                        dve.wait_ge(lat_ready, Count(dst + n - 3).at(l, 3).value())
                for t in range(10, 15):
                    take_root(r)
                    r = r + 1
                    evacuated(dve, PR + t)
                    gain = V_GK if t == 14 else V_GQ
                    v(V.scalar_tensor_tensor(tmp, pj[:, t, :], lvec[:, gain:gain + 1], rs, ALU.mult, ALU.mult))
                    v.sync()
                    dve.sem_inc(passed, 1)
                    v(V.stream_shuffle(hf, tmp, HALF_SWAP))
                    v.sync()
                    v(V.tensor_tensor(tmp, tmp, tab[:, 0, :], ALU.mult))
                    v(V.tensor_tensor(hf, hf, tab[:, 1, :], ALU.mult))
                    v.sync()
                    v(V.tensor_tensor(pj[:, t, :], tmp, hf, ALU.add))
                evacuated(dve, PR + 9)
                v.sync()
                dve.sem_inc(passed, 1)
                v(V.stream_shuffle(hf[64:96, :], pj[64:96, 9, :], HALF_SWAP))
                v.sync()
                v(V.tensor_tensor(hf[64:96, :], hf[64:96, :], tabm[64:96, 1, :], ALU.mult))
                v(V.tensor_tensor(pj[64:96, 9, :], pj[64:96, 9, :], tabm[64:96, 0, :], ALU.mult))
                v.sync()
                v(V.tensor_tensor(pj[64:96, 9, :], pj[64:96, 9, :], hf[64:96, :], ALU.add))
                v.sync()

                def pair(U, masked, tile):
                    B = U.half()
                    for s in range(11):
                        if s < 8:
                            b, h = s // 2, s % 2
                            dve.wait_ge(scores_ready, (U + (s + 1)).value())
                            dve.wait_ge(probs_ready, (U + (s - 1 + C_UNIT)).value())
                            src = ps[:, SC + s % 2, :]
                            if masked is not None:
                                bb = bias[:, bass.ds(masked * 2 + h, 1), 6 - 2 * b:14 - 2 * b, :].rearrange("p a j n -> p (a j n)")
                                v(V.tensor_tensor(sS[:, s % 2, :], src, bb, ALU.add))
                                v.sync()
                                src = sS[:, s % 2, :]
                            V.tensor_reduce(nmax[:, s % 2:s % 2 + 1], src, AX_X, ALU.max, negate=True).then_inc(max_ready, 1)
                        if 2 <= s < 10:
                            u = s - 2
                            b, h = u // 2, u % 2
                            dve.wait_ge(probs_ready, (U + (u + 1 + C_UNIT)).value())
                            dve.wait_ge(pv_done, (U + (u + 1 + C_UNIT)).value())
                            dve.wait_ge(ot_ready, (B + (b - 1)).value()) if b >= 2 else None
                            v(V.reciprocal(rinv[:, u % 4:u % 4 + 1], rsum[:, u % 4:u % 4 + 1]))
                            v.sync()
                            V.tensor_scalar(osb[:, b % 2, 64 * h:64 * h + 64], ps[:, OB + h, 0:64],
                                            rinv[:, u % 4:u % 4 + 1], None, ALU.mult).then_inc(o_used, 1)
                        if s >= 4 and s % 2 == 0:
                            b = s // 2 - 2
                            dve.wait_ge(ot_ready, (B + (b + 1)).value())
                            src = ps[:, ACC + b % 2, 0:P]
                            hi, lo = (oT[:, part, bass.ds(tile, 1), b * P:(b + 1) * P].rearrange("p a n -> p (a n)") for part in (0, 1))
                            v(V.tensor_copy(hi, src))
                            v.sync()
                            V.tensor_tensor(lo, src, hi, ALU.subtract).then_inc(ot_used, 1)

                dve.wait_ge(bias_ready, Count(1).at(l, 1).value())
                for t in (0, 1, 2, 3):
                    evacuated(dve, PR + t)
                with v.loop("na", 2) as i:
                    v(V.tensor_scalar(qst[:, 0, :], pj[:, bass.ds(i, 1), :].rearrange("p a n -> p (a n)"), 0.125, None, ALU.mult))
                    v.sync()
                    V.tensor_copy(kst[:], pj[:, bass.ds(i + 2, 1), :].rearrange("p a n -> p (a n)")).then_inc(stage_ready, 1)
                    pair(Count(0).at(l, 64).at(i, 8), i, i)
                for h in range(4):
                    evacuated(dve, PR + (P_MLA + h))
                for h in range(4):
                    q1 = pj[64:96, h, :]
                    dve.sem_inc(passed, 1)
                    v(V.stream_shuffle(hf[64:96, :], q1, HALF_SWAP))
                    v.sync()
                    v(V.tensor_tensor(hf[64:96, :], hf[64:96, :], tabm[64:96, 1, :], ALU.mult))
                    v(V.tensor_tensor(q1, q1, tabm[64:96, 0, :], ALU.mult))
                    v.sync()
                    v(V.tensor_tensor(q1, q1, hf[64:96, :], ALU.add))
                    v.sync()
                for h in range(4):
                    v(V.tensor_copy(pj[64:96, 4 + h, :], pj[64:96, 9, :]))
                v.sync()
                for h in range(4):
                    evacuated(dve, PR + (P_MLA + 4 + h))
                with v.loop("mla", 2) as i:
                    for h in range(2):
                        ins = V.tensor_scalar(qst[0:96, h, :], pj[0:96, bass.ds(i * 2 + h, 1), :].rearrange("p a n -> p (a n)"),
                                              96 ** -0.5, None, ALU.mult)
                        if h:
                            ins.then_inc(stage_ready, 1)
                        else:
                            v(ins)
                            v.sync()
                    pair(Count(16).at(l, 64).at(i, 8), None, i + 2)
                with v.loop("gqa", 4) as i:
                    V.tensor_scalar(qst[:, 0, :], pj[:, bass.ds(i + 10, 1), :].rearrange("p a n -> p (a n)"), 0.125, None,
                                    ALU.mult).then_inc(stage_ready, 1)
                    pair(Count(32).at(l, 64).at(i, 8), None, i + 4)
                with v.loop("merge", KD) as m:
                    for g in range(3):
                        p = (PR + (P_MERGE + 3 + g)).at(m, 6)
                        evacuated(dve, (PR + (P_MERGE + g)).at(m, 6))
                        if g < 2:
                            dve.wait_ge(part_ready, Count(7 + g).at(l, 22).at(m, 2).value())
                        else:
                            dve.wait_ge(tile_used, (TI + (T_MERGE + 4)).at(m, 4).value())
                        dst = tmp if g == 0 else hf
                        V.scalar_tensor_tensor(dst, sg[:, g, :], 1.0, ps[:, ACC + p.mod(2), :], ALU.add, ALU.mult
                                               ).then_inc(bank_free[p.mod(2)], 1)
                        evacuated(dve, p)
                        if g:
                            v(V.tensor_tensor(tmp, tmp, hf, ALU.add))
                            v.sync()
                    hi, lo = (mg[:, part, bass.ds(m, 1), :].rearrange("p a n -> p (a n)") for part in (0, 1))
                    v(V.tensor_scalar(hi, tmp, 0.5, None, ALU.mult))
                    v.sync()
                    V.scalar_tensor_tensor(lo, tmp, 0.5, hi, ALU.mult, ALU.subtract).then_inc(mg_ready, 1)
                    dve.wait_ge(mg_ready, Count(2).at(l, KD).at(m, 1).value())
                with v.loop("out", 2) as i:
                    for u in range(4):
                        residual((TI + (T_OUT + u)).at(i, 4), (PR + (P_OUT + u)).at(i, 4), i * 4 + u, G_M)
                for k in range(KD):
                    evacuated(dve, PR + (P_OUT + k))
                norm(R + 8, H + KD, 1, SH_F)
                dve.wait_ge(h_ready, (H + 2 * KD).value())
                with v.loop("gu", KF // 2) as i:
                    for j in range(2):
                        t, p = (TI + (T_GU + 2 * j)).at(i, 4), (PR + (P_GU + 2 * j)).at(i, 4)
                        dve.wait_ge(up_tanh, Count(j + 1).at(l, KF).at(i, 2).value())
                        V.scalar_tensor_tensor(tmp, tg[:, j, :], 1.0, ps[:, ACC, :], ALU.add, ALU.mult).then_inc(bank_free[0], 1)
                        evacuated(dve, p)
                        dve.wait_ge(tile_used, (t + 2).value())
                        V.scalar_tensor_tensor(hf, ps[:, ACC + 1, :], 0.5, tmp, ALU.mult, ALU.mult).then_inc(bank_free[1], 1)
                        evacuated(dve, p + 1)
                        hi, lo = (act_f[:, part, bass.ds(i * 2 + j, 1), :].rearrange("p a n -> p (a n)") for part in (0, 1))
                        split(hi, lo, hf, act_ready)
                        dve.wait_ge(act_ready, Count(j + 1 + C_UNIT).at(l, KF).at(i, 2).value())
                with v.loop("down", 2) as i:
                    for u in range(4):
                        residual((TI + (T_DOWN + 3 * u + 2)).at(i, 12), (PR + (P_DOWN + u)).at(i, 4), i * 4 + u, G_F)
                for k in range(KD):
                    evacuated(dve, PR + (P_DOWN + k))
            Q0, R0, H0 = 24 * DEPTH + KD, 9 * DEPTH + 1, 2 * KD * DEPTH
            TT, TS, STT = V.tensor_tensor, V.tensor_scalar, V.scalar_tensor_tensor
            dve.sem_inc(m_done, 1)
            dve.sem_inc(shifted, 2)
            dve.sem_inc(mlp_ready, C_UNIT)
            v(V.tensor_copy(gs[:, 0, :], vecx[:, X_N1:X_N1 + KD]))
            v(V.tensor_copy(gs[:, 1, :], vecx[:, X_N2:X_N2 + KD]))
            v(V.memset(lm[:, 0:KD], 0.0))
            v.sync()
            take_root(Count(R0 - 1))
            for k in range(KD):
                STT(xT[:, k, :], xT[:, k, :], vecx[:, X_F1 + k:X_F1 + k + 1], rs, ALU.mult, ALU.mult).then_inc(xf_ready, 1)
            dve.wait_ge(xf_ready, KD)
            norm(Count(R0), Count(H0), 0, 0)
            dve.wait_ge(s_in2, 32)
            v(TS(half2[:], vec2[:], 0.5, None, ALU.mult))
            v(STT(sp[:, 0, :], vec2[:, :, W_AP], -1.0, vec2[:, :, W_AP], ALU.mult, ALU.max))
            v.sync()
            V.tensor_scalar(k1[:], half2[:, :, W_KA], -1.0, 1.0, ALU.mult, ALU.add).then_inc(sp_abs, 1)
            v(V.memset(shf[:, :, 0:3], 0.0))
            v(V.memset(dB[:, :, 0:1], 0.0))
            dve.wait_ge(sp_exp, 1)
            V.tensor_scalar(sp[:, 2, :], sp[:, 1, :], 1.0, None, ALU.add).then_inc(sp_w, 1)
            dve.wait_ge(sp_ln, 1)
            dve.wait_ge(sp_w, 1)
            v(TS(sp[:, 4, :], sp[:, 2, :], 1.0, None, ALU.subtract))
            v.sync()
            v(TS(sp[:, 5, :], sp[:, 4, :], 0.0, None, ALU.is_equal))
            v.sync()
            v(TT(sp[:, 4, :], sp[:, 4, :], sp[:, 5, :], ALU.add))
            v(TT(sp[:, 3, :], sp[:, 3, :], sp[:, 5, :], ALU.add))
            v.sync()
            v(V.reciprocal(sp[:, 4, :], sp[:, 4, :]))
            v(TT(sp[:, 3, :], sp[:, 3, :], sp[:, 1, :], ALU.mult))
            v.sync()
            v(TT(sp[:, 3, :], sp[:, 3, :], sp[:, 4, :], ALU.mult))
            v.sync()
            v(STT(sp[:, 6, :], vec2[:, :, W_AP], 0.0, sp[:, 3, :], ALU.max, ALU.add))
            v.sync()
            v(TS(sp[:, 6, :], sp[:, 6, :], -4.0, None, ALU.mult))
            v.sync()

            def shift(dst, j, mu, signal, count):
                v(TT(tmp, shf[:, j, 2:S + 2], shf[:, j, 3:S + 3], ALU.subtract))
                v.sync()
                STT(dst, tmp, mu, shf[:, j, 3:S + 3], ALU.mult, ALU.add).then_inc(signal, 1)
                dve.wait_ge(signal, count.value())

            for j, dst in enumerate((kB, vB)):
                evacuated(dve, Count(P_B2 + j))
                shift(dst[:], j, vecx[:, X_MU + j:X_MU + j + 1], xw_ready, Count(j + 1))
            dve.wait_ge(xw_tanh, 2)
            dve.wait_ge(xw_ready, 2)
            v(TS(vB[:], vB[:], 1.0, 0.5, ALU.add, ALU.mult))
            v(V.tensor_copy(hf, kB[:]))
            v.sync()
            split(xaR[:, 0, :], xaR[:, 1, :], hf, xin_ready)
            split(xgR[:, 0, :], xgR[:, 1, :], vB[:], xin_ready)
            dve.wait_ge(xin_ready, 2)
            v.sync()
            dve.sem_inc(vec2_ready, 1)
            with v.loop("m", KD) as m:
                Pm, Tm = Count(P_B2 + 2).at(m, P_M), Count(T_B2 + 2).at(m, T_M)

                def vec(table, col):
                    return table[:, bass.ds(m, 1), col:col + 1].rearrange("p a n -> p (a n)")

                def col(table, *at):
                    return table[(slice(None), *at, bass.ds(m, 1))]

                def once(sem_, n=1, per=1, of=0):
                    dve.wait_ge(sem_, Count(n + of).at(m, per).value())

                evacuated(dve, Pm)
                shift(kB[:], 0, vec(vec2, W_MUK), shifted, Count(1 + 2).at(m, 5))
                TS(kkB[:], kB[:], vec(vec2, W_KK), None, ALU.mult).then_inc(kk_ready, 1)
                evacuated(dve, Pm + 1)
                shift(vB[:], 1, vec(vec2, W_MUV), shifted, Count(2 + 2).at(m, 5))
                evacuated(dve, Pm + 2)
                shift(rB[:], 0, vec(vec2, W_MUR), shifted, Count(3 + 2).at(m, 5))
                evacuated(dve, Pm + 3)
                v(TS(hf, shf[:, 1, 0:S], vec(vec2, W_CW), vec(vec2, W_CB), ALU.mult, ALU.add))
                v.sync()
                for j in range(1, 4):
                    ins = STT(hf, shf[:, 1, j:j + S], vec(vec2, W_CW + j), hf, ALU.mult, ALU.add)
                    if j < 3:
                        v(ins)
                        v.sync()
                    else:
                        ins.then_inc(shifted, 1)
                once(shifted, 4 + 2, 5)
                split(uR[:, 0, :], uR[:, 1, :], hf, u_ready)
                evacuated(dve, Pm + 4)
                v(TS(tmp.rearrange("p (a n) -> p a n", a=CH), e1[:, :, 0:P], 1.0, RATE / 2, ALU.add, ALU.mult))
                v(V.memset(dB[:, :, 0:1], 0.0))
                v.sync()
                for cc in range(CH):
                    v(V.tensor_tensor_scan(dB[:, cc, 1:P + 1], ones[:], tmp[:, cc * P:(cc + 1) * P], 0.0, ALU.mult, ALU.add))
                v.sync()
                v(V.tensor_copy(mid[:], dB[:, :, P // 2]))
                v.sync()
                TT(dB[:], dB[:], mid[:].unsqueeze(2).broadcast_to([P, CH, P + 1]), ALU.subtract).then_inc(d_ready, 1)
                evacuated(dve, Pm + 7)
                evacuated(dve, Pm + 8)
                TS(sg2[:, 0, :], sg2[:, 0, :], 1.0, col(sp, 6), ALU.add, ALU.mult).then_inc(la_ready, 1)
                once(u_ready)
                v(STT(hf, sg2[:, 1, :], 1.0, hf, ALU.add, ALU.mult))
                once(lru_ex, 2, 2)
                v(TS(tmp, yB[:], 1.0, None, ALU.add))
                v.sync()
                v(V.reciprocal(tmp, tmp))
                v.sync()
                STT(yB[:], yB[:], 2.0, tmp, ALU.mult, ALU.mult).then_inc(lq_ready, 1)
                once(lmul_ready)
                v(V.memset(yB[:, 0:1], 1.0))
                v.sync()
                v(STT(hf, hf, 0.5, yB[:], ALU.mult, ALU.mult))
                v.sync()
                V.tensor_tensor_scan(tmp, sg2[:, 2, :], hf, 0.0, ALU.mult, ALU.add).then_inc(lru_done, 1)
                once(lru_done)
                v(V.tensor_copy(hf, tmp))
                evacuated(dve, Pm + 9)
                dve.wait_ge(tile_used, (Tm + 7).value())
                STT(shf[:, 0, 3:S + 3], msum, 1.0, ps[:, ACC, :], ALU.mult, ALU.mult).then_inc(bank_free[0], 1)
                evacuated(dve, Pm + 10)
                v(TS(tmp, shf[:, 0, 1:S + 1], vec(vec2, W_CA), None, ALU.mult))
                v.sync()
                v(STT(tmp, shf[:, 0, 2:S + 2], vec(vec2, W_CA + 1), tmp, ALU.mult, ALU.add))
                v.sync()
                STT(tmp, shf[:, 0, 3:S + 3], vec(vec2, W_CA + 2), tmp, ALU.mult, ALU.add).then_inc(shifted, 1)
                once(shifted, 5 + 2, 5)
                dve.wait_ge(tile_used, (Tm + 8).value())
                TT(tmp, tmp, ps[:, ACC + 1, :], ALU.mult).then_inc(bank_free[1], 1)
                evacuated(dve, Pm + 11)
                evacuated(dve, Pm + 13)
                v(STT(msum, sg2[:, 0, :], 1.0, tmp, ALU.add, ALU.mult))
                evacuated(dve, Pm + 12)
                v(TT(hf, hf, yB[:], ALU.mult))
                v.sync()
                evacuated(dve, Pm + 14)
                v(STT(hf, sg2[:, 1, :], 1.0, hf, ALU.add, ALU.mult))
                v.sync()
                v(TT(msum, msum, hf, ALU.add))
                dve.wait_ge(root_ready, Count(R0 + 2).at(m, 2).value())
                v(TS(rs, rt, 1e-12, None, ALU.max))
                v.sync()
                V.reciprocal(rs, rs).then_inc(root_used, 1)
                dve.wait_ge(root_used, Count(R0 + 3).at(m, 2).value())
                evacuated(dve, Pm + 5)
                evacuated(dve, Pm + 6)
                once(e_ready, 2, 2)
                ch = lambda b: b.rearrange("p (a n) -> p a n", a=CH)
                v(TS(tmp, aB[:], vec(half2, W_KA), col(k1), ALU.mult, ALU.add))
                v(TT(kkB[:], kkB[:], rs, ALU.mult))
                v.sync()
                v(TT(kB[:], kB[:], tmp, ALU.mult))
                v(STT(aB[:], aB[:], 1.0, kkB[:], ALU.add, ALU.mult))
                v.sync()
                v(STT(bnB[:], rB[:], vec(vec2, W_RK), kB[:], ALU.mult, ALU.mult))
                v(STT(ch(aB[:]), ch(aB[:]), 0.5, e2[:, :, 1:P + 1], ALU.mult, ALU.mult))
                v.sync()
                v(TT(ch(kB[:]), ch(kB[:]), e2[:, :, 1:P + 1], ALU.mult))
                v(TT(ch(rB[:]), ch(rB[:]), e1[:, :, 1:P + 1], ALU.mult))
                v.sync()
                STT(ch(kkB[:]), ch(kkB[:]), -1.0, e1[:, :, 0:P], ALU.mult, ALU.mult).then_inc(prep_ready, 1)
                for n, (kind, h, lv) in enumerate(RW):
                    if (kind, h, lv) == ("X", 0, 1):
                        v.sync()
                    once(mat_ready, n + 1, len(RW))
                    src = ps[:, RW_BANK[kind] + h, :].rearrange("p (a n) -> p a n", a=CH)
                    if kind in ("LT", "MT", "GB", "GK"):
                        mask = lev[:, LEVELS + (2 if kind in ("LT", "MT") else 3), :]
                        TT(mats[kind][:, h], src, mask.unsqueeze(1).broadcast_to([P, CH, P]), ALU.mult).then_inc(mat_used, 1)
                        if kind == "LT":
                            once(mat_used, n + 1, len(RW))
                            v(TT(mats["TT"][:, h], mats["LT"][:, h], lev[:, LEVELS + 1, :].unsqueeze(1).broadcast_to([P, CH, P]), ALU.mult))
                            v.sync()
                            v(TT(mats["TT"][:, h], mats["TT"][:, h], ident[:].unsqueeze(1).broadcast_to([P, CH, P]), ALU.add))
                    elif kind == "L":
                        v(TT(mats["T"][:, h], src, lev[:, 0, :].unsqueeze(1).broadcast_to([P, CH, P]), ALU.mult))
                        v.sync()
                        TT(mats["T"][:, h], mats["T"][:, h], ident[:].unsqueeze(1).broadcast_to([P, CH, P]), ALU.add).then_inc(mat_used, 1)
                    elif kind == "X":
                        TT(mats["X"][:, h], src, lev[:, lv, :].unsqueeze(1).broadcast_to([P, CH, P]), ALU.mult).then_inc(mat_used, 1)
                    else:
                        TT(mats[kind][:, h], src, mats[kind][:, h], ALU.add).then_inc(mat_used, 1)
                v.sync()
                once(mat_used, len(RW), len(RW))
                for cc in range(CH - 1):
                    for h in range(2):
                        rows_ = slice(64 * h, 64 * h + 64)
                        new, old = state[rows_, (cc + 1) % 2, :], state[rows_, cc % 2, :]
                        once(st_psum, 2 * cc + h + 1, 6)
                        src = ps[rows_, 7, 0:64]
                        if cc:
                            v(TT(new, src, old, ALU.add))
                            v.sync()
                            src = new
                        TS(new, src, e1[rows_, cc, P:P + 1], e2[rows_, cc + 1, 0:1], ALU.mult, ALU.mult).then_inc(st_sb, 1)
                        once(st_sb, 2 * cc + h + 1, 6)
                once(bn_sum)
                v(TT(vB[:], vB[:], ps[:, 3, :], ALU.mult))
                once(mean_ready)
                once(y_sb)
                STT(yB[:], ps[:, 2, :], -1.0 / 64, yB[:], ALU.mult, ALU.add).then_inc(yc_ready, 1)
                once(yc_ready)
                take_root(Count(R0 + 2).at(m, 2))
                v(TT(yB[:], yB[:], rs, ALU.mult))
                v.sync()
                v(TS(yB[:], yB[:], vec(vec2, W_LG), vec(vec2, W_LB), ALU.mult, ALU.add))
                v.sync()
                v(TT(yB[:], yB[:], vB[:], ALU.add))
                v.sync()
                v(TT(yB[:], yB[:], gB[:], ALU.mult))
                v.sync()
                evacuated(dve, Pm + 15)
                v(STT(yB[:], sg2[:, 2, :], 1.0, yB[:], ALU.add, ALU.mult))
                v.sync()
                v(TT(msum, msum, yB[:], ALU.add))
                v.sync()
                hi, lo = (mR[:, part, bass.ds(m, 1), :].rearrange("p a n -> p (a n)") for part in (0, 1))
                v(TS(hi, msum, 0.5, None, ALU.mult))
                v.sync()
                STT(lo, msum, 0.5, hi, ALU.mult, ALU.subtract).then_inc(m_done, 1)
                once(m_done, 2)
            def plain_residual(t, p, m_):
                dve.wait_ge(tile_used, (t + 1).value())
                xm = xT[:, bass.ds(m_, 1), :].rearrange("p a n -> p (a n)") if not isinstance(m_, int) else xT[:, m_, :]
                TT(xm, ps[:, ACC + p.mod(2), :], xm, ALU.add).then_inc(bank_free[p.mod(2)], 1)

            for u in range(KD):
                plain_residual(Count(T_OUT2 + u), Count(P_OUT2 + u), u)
            for k in range(KD):
                evacuated(dve, Count(P_OUT2 + k))
            R1 = R0 + 1 + 2 * KD
            norm(Count(R1), Count(H0 + KD), 1, 0)
            v.sync()
            dve.wait_ge(h_ready, H0 + 2 * KD)
            with v.loop("mlp", 2) as hh:
                with v.loop("mlp1", 4) as i:
                    for u in range(4):
                        p = Count(P_MLP + u).at(hh, 24).at(i, 4)
                        dve.wait_ge(relu_ready, Count(u + 1).at(hh, 16).at(i, 4).value())
                        TT(hf, relu[:, u % 2, :], ps[:, ACC + u % 2, :], ALU.mult).then_inc(bank_free[u % 2], 1)
                        evacuated(dve, p)
                        hi, lo = (mlpR[:, part, bass.ds(i * 4 + u, 1), :].rearrange("p a n -> p (a n)") for part in (0, 1))
                        split(hi, lo, hf, mlp_ready)
                        dve.wait_ge(mlp_ready, Count(u + 1 + C_UNIT).at(hh, 16).at(i, 4).value())
                with v.loop("mlp2", 4) as i:
                    for u in range(2):
                        plain_residual(Count(T_MLP + 17 + 2 * u).at(hh, 32).at(i, 4), Count(P_MLP + 16 + u).at(hh, 24).at(i, 2), i * 2 + u)
                for k in range(KD):
                    evacuated(dve, Count(P_MLP + 16 + k).at(hh, 24))
            take_root(Count(R1 + 1))
            for k in range(KD):
                STT(xT[:, k, :], xT[:, k, :], vecx[:, X_FIN + k:X_FIN + k + 1], rs, ALU.mult, ALU.mult).then_inc(fin_ready, 1)


def tile_of(w, np):
    k, n = w.shape
    t = w.reshape(k // P, P, n).transpose(1, 0, 2).reshape(P, -1)
    return np.concatenate([t, np.zeros((P, 1024 - t.shape[1]), t.dtype)], 1)[None]


def tiles_of(w, np):
    k, n = w.shape
    return w.reshape(KD, P, n // P, P).transpose(2, 1, 0, 3).reshape(n // P, P, 1024)


def columns(v):
    return v.reshape(-1, P).T


def first_weights(a, np):
    out = []
    for l in range(DEPTH):
        w = a["w_in"][l]
        out += [tiles_of(w[:, :1152], np), tiles_of(w[:, 1088:1216], np)]
        gq = w[:, 1184:1696].reshape(D, 2, 4, 64).transpose(0, 2, 1, 3).reshape(D, 512)
        out += [tiles_of(gq, np), tiles_of(w[:, 1696:1952], np)]
        uq = a["mla_w_uq"][l]
        out += [tile_of(uq[:, :192], np), tile_of(uq[:, 192:], np)]
        ukv = a["mla_w_ukv"][l].reshape(P, 4, 2, 64)
        out += [tile_of(ukv[:, :, 0].reshape(P, 256), np), tile_of(ukv[:, :, 1].reshape(P, 256), np)]
        gates = [tiles_of(w[:, 1952 + D * g:1952 + D * (g + 1)], np) for g in range(3)]
        br = np.concatenate([a["w_br_na"][l], a["w_br_mla"][l],
                             a["w_br_gqa"][l].reshape(2, 4, 64, D).transpose(1, 0, 2, 3).reshape(512, D)], 0)
        out.append(np.stack(gates + [tiles_of(br, np)], 1).reshape(-1, P, 1024))
        out.append(tiles_of(a["w_out"][l], np))
        gu = a["ffn_w_gate_up"][l]
        out.append(np.stack([tiles_of(gu[:, :FFN], np), tiles_of(gu[:, FFN:], np)], 1).reshape(-1, P, 1024))
        down = np.concatenate([a["ffn_w_down"][l], np.zeros((3 * 1024 - FFN, D), gu.dtype)], 0)
        out.append(np.stack([tiles_of(down[1024 * t:1024 * (t + 1)], np) for t in range(3)], 1).reshape(-1, P, 1024))
    return out


def second_weights(a, np):
    w = a["w_in_2"][0]
    rwkv = 8 * D
    col = lambda start: tiles_of(w[:, start:start + D], np)
    out = [tiles_of(w[:, rwkv + 3 * D:rwkv + 3 * D + 256], np)]
    lru = []
    for name in ("lru_wa_2", "lru_wi_2"):
        g = a[name][0].reshape(KD, 2, 64, 64)
        full = np.zeros((KD, 2, 64, 2, 64), g.dtype)
        full[:, 0, :, 0], full[:, 1, :, 1] = g[:, 0], g[:, 1]
        lru.append(full.reshape(KD, P, P))
    wa = np.concatenate([a["rwkv_w2_2"][0], a["rwkv_a2_2"][0]], 0).reshape(P, KD, P).transpose(1, 0, 2)
    g2 = a["rwkv_g2_2"][0].reshape(P, KD, P).transpose(1, 0, 2)
    small = np.concatenate([wa, g2] + lru + [np.zeros((KD, P, 512), w.dtype)], 2)
    per = [col(rwkv + D), col(rwkv + 2 * D), col(rwkv), col(3 * D), small, col(D), col(2 * D), col(0), col(4 * D)]
    per += [col(5 * D + g * D) for g in range(3)]
    out.append(np.stack(per, 1).reshape(-1, P, 1024))
    out.append(tiles_of(a["w_out_2"][0], np))
    w1, w2 = a["mlp_w1_2"][0], a["mlp_w2_2"][0]
    for hh in range(2):
        out.append(tiles_of(w1[:, 2048 * hh:2048 * (hh + 1)], np))
        down = w2[2048 * hh:2048 * (hh + 1)]
        out.append(np.stack([tiles_of(down[:1024], np), tiles_of(down[1024:], np)], 1).reshape(-1, P, 1024))
    out.append(np.zeros((T_TOTAL - T_USED, P, 1024), w.dtype))
    return out


def rope_table(pos, half, np):
    inv = (1.0 / (np.float32(10000.0) ** (np.arange(half, dtype=np.float32) / np.float32(half)))).astype(np.float32)
    ang = (pos.astype(np.float32)[None, :] * inv[:, None]).astype(np.float32)
    cos, sin = np.cos(ang), np.sin(ang)
    return np.concatenate([cos, cos], 0), np.concatenate([-sin, sin], 0)


def constants(np):
    t = np.arange(S)
    rc, rsn = rope_table(t // GRID, 16, np)
    cc, csn = rope_table(t % GRID, 16, np)
    axial = np.stack([np.concatenate([rc, cc] * 2, 0), np.concatenate([rsn, csn] * 2, 0)], 1)
    mc, ms = rope_table(t, 16, np)
    rope = np.zeros((P, 2, S), np.float32)
    rope[64:96, 0], rope[64:96, 1] = mc, ms
    q, k = np.arange(P)[:, None] % GRID, np.arange(GRID)[None]
    start = np.clip(q - 8, 0, GRID - 16)
    mask = np.where((k >= start) & (k < start + 16), 0.0, -1e30)
    half = np.arange(P) // 64
    i, j = np.arange(P)[:, None], np.arange(P)[None]
    levels = [(i >> (lv + 1) == j >> (lv + 1)) & (i >> lv & 1 == 1) & (j >> lv & 1 == 0) for lv in range(LEVELS + 1)]
    levels = np.stack(levels + [levels[0].T, i < j, i <= j], 1)
    named = {"levels": levels, "axial": axial, "rope": rope, "colmask": mask, "ident": np.eye(P), "blk": half[:, None] == half[None]}
    return {k: v.astype(np.float32) for k, v in named.items()}


def kernel(**inputs):
    import numpy as np
    import concourse.bacc as bacc
    from concourse.bass_utils import run_bass_kernel_spmd

    a = {k: np.asarray(v) for k, v in inputs.items()}
    ada = np.concatenate([a["ada_w"][l].T.reshape(-1, P, D) for l in range(DEPTH)], 0)
    stream = np.concatenate([ada] + first_weights(a, np) + second_weights(a, np), 0)
    vec1 = np.concatenate([columns(v) for l in range(DEPTH) for v in (
        a["norm_mix_g"][l], a["norm_ffn_g"][l], a["mla_q_norm_g"][l], a["mla_kv_norm_g"][l],
        np.concatenate([a["gqa_q_norm_g"][l]] * 2), np.concatenate([a["gqa_k_norm_g"][l]] * 2))], 1)
    mu = a["rwkv_mu_2"][0]
    per_tile = [mu[D:2 * D], mu[2 * D:3 * D], mu[:D], a["rwkv_w0_2"][0], a["rwkv_a0_2"][0], a["rwkv_kk_2"][0], a["rwkv_ka_2"][0],
                a["rwkv_rk_2"][0].reshape(D), a["rwkv_lnx_g_2"][0], a["rwkv_lnx_b_2"][0], a["lru_conv_b_2"][0],
                *a["lru_conv_w_2"][0], a["lru_ba_2"][0], a["lru_bi_2"][0], a["lru_a_param_2"][0], *a["conv_a_w_2"][0],
                *a["merge_b_2"][0].reshape(3, D)]
    vec2 = np.stack([columns(v) for v in per_tile], 2)
    vecx = np.concatenate([columns(v) for v in (a["norm1_g_2"][0], a["norm2_g_2"][0], a["final_g_2"], mu[3 * D:], a["final_norm_g"])], 1)
    arrays = {
        "x": a["x"][0].T.reshape(KD, P, S).transpose(1, 0, 2), "c": a["c"].reshape(1, D), "weights": stream,
        "ada_b": columns(a["ada_b"]), "vec1": vec1, "rpb": a["na_rpb"].reshape(DEPTH * 60, 31),
        "vec2": vec2, "vecx": vecx,
    }
    tables = constants(np)
    nc = bacc.Bacc("TRN2", target_bir_lowering=False, num_devices=1, dynamic_dma_scratch_size=2048)
    arrays = {f"in_{k}_dram": np.ascontiguousarray(v) for k, v in arrays.items()}
    tabs = {f"in_{k}_dram": np.ascontiguousarray(v) for k, v in tables.items()}
    aps = {k: nc.dram_tensor(k, v.shape, mybir.dt.from_np(v.dtype), kind="ExternalInput").ap()
           for k, v in list(arrays.items()) + list(tabs.items())}
    out = nc.dram_tensor("out_0_dram", (P, KD, S), F32, kind="ExternalOutput").ap()
    build(nc, *[aps[k] for k in arrays], {k: aps[f"in_{k}_dram"] for k in tables}, out)
    r = run_bass_kernel_spmd(nc, [{**arrays, **tabs}], core_ids=[0])
    got = r.results[0]["out_0_dram"]
    return np.ascontiguousarray(got.transpose(1, 0, 2).reshape(D, S).T)[None]
```
